# Optimizing a Trainium2 kernel written in Bass

```python
import jax
import jax.numpy as jnp
from jax import lax
import numpy as np

D_MODEL = 1024
BATCH = 1
SEQ = 1024
DEPTH = 1
DEC_BATCH = 1
DEC_SEQ = 32
PAST_LEN = 512

CHUNK = 64
NORM_EPS = 1e-6
ML_HEADS = 4
ML_HEAD_DIM = 128
ML_WIDTH = ML_HEADS * ML_HEAD_DIM
SWA_HEADS = 8
SWA_KV_HEADS = 2
SWA_GROUP = SWA_HEADS // SWA_KV_HEADS
SWA_HEAD_DIM = 64
SWA_WIDTH = SWA_HEADS * SWA_HEAD_DIM
SWA_KV_WIDTH = SWA_KV_HEADS * SWA_HEAD_DIM
WINDOW = 128
WINDOW_CHUNKS = WINDOW // CHUNK
ROPE_THETA = 500000.0
ROPE_DIM = SWA_HEAD_DIM // 4
MIX_WIDTH = ML_WIDTH + SWA_WIDTH
IN_SPLITS = (ML_WIDTH, 2 * ML_WIDTH, 3 * ML_WIDTH, 4 * ML_WIDTH, 4 * ML_WIDTH + ML_HEADS, 4 * ML_WIDTH + 2 * ML_HEADS, 4 * ML_WIDTH + 2 * ML_HEADS + SWA_WIDTH, 4 * ML_WIDTH + 2 * ML_HEADS + SWA_WIDTH + SWA_KV_WIDTH)
IN_COLS = 4 * ML_WIDTH + 2 * ML_HEADS + SWA_WIDTH + 2 * SWA_KV_WIDTH
PEER_HEADS = 8
N_KEYS = 128
N_EXPERTS = N_KEYS * N_KEYS
PEER_TOPK = 16
PEER_KEY_DIM = 256
PEER_HALF = PEER_KEY_DIM // 2
PEER_BLOCK = 128

kernel_name = "hymba_mlstm_swa_peer_stream_step"

def rmsnorm(x, w):
    xf = x.astype(jnp.float32)
    y = xf * lax.rsqrt(jnp.mean(xf * xf, axis=-1, keepdims=True) + NORM_EPS)
    return (y * w.astype(jnp.float32)).astype(x.dtype)

def head_rmsnorm(h, w):
    B, T, H, Dh = h.shape
    hf = h.astype(jnp.float32)
    y = hf * lax.rsqrt(jnp.mean(hf * hf, axis=-1, keepdims=True) + NORM_EPS)
    return y.reshape(B, T, H * Dh) * w.astype(jnp.float32)

def rope(x, pos):
    half = ROPE_DIM // 2
    inv = ROPE_THETA ** (-jnp.arange(half, dtype=jnp.float32) * 2.0 / ROPE_DIM)
    ang = pos.astype(jnp.float32)[:, None] * inv[None, :]
    cos = jnp.cos(ang)[:, None, :]
    sin = jnp.sin(ang)[:, None, :]
    xf = x.astype(jnp.float32)
    x1 = xf[..., :half]
    x2 = xf[..., half:ROPE_DIM]
    out = jnp.concatenate([x1 * cos - x2 * sin, x2 * cos + x1 * sin, xf[..., ROPE_DIM:]], axis=-1)
    return out.astype(x.dtype)

def mlstm_chunk(carry, inp):
    c, n, m = carry
    q, k, v, ig, lf = inp
    L = q.shape[2]
    b = jnp.cumsum(lf, axis=-1)
    causal = jnp.tril(jnp.ones((L, L), dtype=bool))
    logd = jnp.where(causal, b[..., :, None] - b[..., None, :] + ig[..., None, :], -jnp.inf)
    m_inter = b + m[..., None]
    m_t = jnp.maximum(m_inter, jnp.max(logd, axis=-1))
    dmat = jnp.exp(logd - m_t[..., None])
    w_inter = jnp.exp(m_inter - m_t)
    qk = jnp.einsum('bhtd,bhsd->bhts', q, k) * dmat
    num = w_inter[..., None] * jnp.einsum('bhed,bhtd->bhte', c, q) + jnp.einsum('bhts,bhse->bhte', qk, v)
    den = w_inter * jnp.einsum('bhd,bhtd->bht', n, q) + jnp.sum(qk, axis=-1)
    h = num / jnp.maximum(jnp.abs(den), jnp.exp(-m_t))[..., None]
    b_last = b[..., -1]
    logw = b_last[..., None] - b + ig
    m_new = jnp.maximum(b_last + m, jnp.max(logw, axis=-1))
    w_s = jnp.exp(logw - m_new[..., None])
    decay = jnp.exp(b_last + m - m_new)
    c_new = decay[..., None, None] * c + jnp.einsum('bhs,bhse,bhsd->bhed', w_s, v, k)
    n_new = decay[..., None] * n + jnp.einsum('bhs,bhsd->bhd', w_s, k)
    return (c_new, n_new, m_new), h

def mlstm_scan(q, k, v, ig, lf, c0, n0, m0, chunk_len):
    f32 = jnp.float32
    B, T, H, Dh = q.shape
    nc = T // chunk_len

    def to_chunks(a):
        a = a.astype(f32).reshape((B, nc, chunk_len) + a.shape[2:])
        return jnp.moveaxis(jnp.moveaxis(a, 3, 2), 1, 0)

    carry0 = (c0.astype(f32), n0.astype(f32), m0.astype(f32))
    (c, n, m), h = lax.scan(mlstm_chunk, carry0, (to_chunks(q), to_chunks(k), to_chunks(v), to_chunks(ig), to_chunks(lf)))
    h = jnp.swapaxes(jnp.moveaxis(h, 0, 1), 2, 3).reshape(B, T, H, Dh)
    return h, c, n, m

def sink_softmax(s, sinks):
    sk = sinks.astype(jnp.float32).reshape(SWA_KV_HEADS, SWA_GROUP, 1, 1)
    mx = jnp.maximum(jnp.max(s, axis=-1, keepdims=True), sk)
    p = jnp.exp(s - mx)
    return p / (jnp.sum(p, axis=-1, keepdims=True) + jnp.exp(sk - mx))

def swa_prompt(q, k, v, sinks):
    B, S = q.shape[:2]
    nc = S // CHUNK
    scale = SWA_HEAD_DIM ** -0.5
    qc = q.reshape(B, nc, CHUNK, SWA_KV_HEADS, SWA_GROUP, SWA_HEAD_DIM)
    pad = ((0, 0), (WINDOW, 0), (0, 0), (0, 0))
    kp = jnp.pad(k, pad).reshape(B, nc + WINDOW_CHUNKS, CHUNK, SWA_KV_HEADS, SWA_HEAD_DIM)
    vp = jnp.pad(v, pad).reshape(B, nc + WINDOW_CHUNKS, CHUNK, SWA_KV_HEADS, SWA_HEAD_DIM)
    kw = jnp.concatenate([kp[:, j:j + nc] for j in range(WINDOW_CHUNKS + 1)], axis=2)
    vw = jnp.concatenate([vp[:, j:j + nc] for j in range(WINDOW_CHUNKS + 1)], axis=2)
    key_chunk = jnp.arange(nc)[:, None] - WINDOW_CHUNKS + (jnp.arange(WINDOW + CHUNK) // CHUNK)[None, :]
    valid = (key_chunk >= 0)[None, :, None, None, None, :]
    s = jnp.einsum('bctkgd,bcskd->bckgts', qc, kw).astype(jnp.float32) * scale
    s = jnp.where(valid, s, -jnp.inf)
    p = sink_softmax(s, sinks).astype(v.dtype)
    o = jnp.einsum('bckgts,bcskd->bctkgd', p, vw)
    return o.reshape(B, S, SWA_WIDTH)

def swa_sample(q, k_all, v_all, sinks):
    B, T = q.shape[:2]
    scale = SWA_HEAD_DIM ** -0.5
    qg = q.reshape(B, T, SWA_KV_HEADS, SWA_GROUP, SWA_HEAD_DIM)
    s = jnp.einsum('btkgd,bskd->bkgts', qg, k_all).astype(jnp.float32) * scale
    p = sink_softmax(s, sinks).astype(v_all.dtype)
    o = jnp.einsum('bkgts,bskd->btkgd', p, v_all)
    return o.reshape(B, T, SWA_WIDTH)

def peer(xblocks, w_q, sub_keys_1, sub_keys_2, expert_u, expert_v):
    def block(xb):
        TB = xb.shape[0]
        q = (xb @ w_q).reshape(TB, PEER_HEADS, PEER_KEY_DIM)
        s1 = jnp.einsum('thd,nd->thn', q[..., :PEER_HALF], sub_keys_1)
        s2 = jnp.einsum('thd,nd->thn', q[..., PEER_HALF:], sub_keys_2)
        t1, i1 = lax.top_k(s1, PEER_TOPK)
        t2, i2 = lax.top_k(s2, PEER_TOPK)
        cand = (t1[..., :, None] + t2[..., None, :]).reshape(TB, PEER_HEADS, PEER_TOPK * PEER_TOPK)
        cidx = (i1[..., :, None] * N_KEYS + i2[..., None, :]).reshape(TB, PEER_HEADS, PEER_TOPK * PEER_TOPK)
        top, sel = lax.top_k(cand, PEER_TOPK)
        idx = jnp.take_along_axis(cidx, sel, axis=-1)
        g = jax.nn.softmax(top.astype(jnp.float32), axis=-1).astype(xb.dtype)
        u = jnp.take(expert_u, idx, axis=0)
        a = jax.nn.gelu(jnp.einsum('thkd,td->thk', u, xb), approximate=False)
        ve = jnp.take(expert_v, idx, axis=0)
        return jnp.einsum('thk,thkd->td', g * a, ve)
    return lax.map(block, xblocks)

def layer(x, pos, prompt, k_cache, v_cache, c0, n0, m0,
          norm_mix_w, w_in, mlstm_if_bias, mlstm_norm_w, swa_sinks, w_out,
          norm_ffn_w, peer_w_q, peer_sub_keys_1, peer_sub_keys_2, peer_u, peer_v):
    f32 = jnp.float32
    B, T, _ = x.shape
    h = rmsnorm(x, norm_mix_w)
    proj = h @ w_in
    mq, mk, mv, mo, mi, mf, sq, sk, sv = jnp.split(proj, IN_SPLITS, axis=-1)
    mshape = (B, T, ML_HEADS, ML_HEAD_DIM)
    gate = jnp.concatenate([mi, mf], axis=-1).astype(f32) + mlstm_if_bias.astype(f32)
    ig = gate[..., :ML_HEADS]
    lf = jax.nn.log_sigmoid(gate[..., ML_HEADS:])
    if prompt:
        c0 = jnp.zeros((B, ML_HEADS, ML_HEAD_DIM, ML_HEAD_DIM), f32)
        n0 = jnp.zeros((B, ML_HEADS, ML_HEAD_DIM), f32)
        m0 = jnp.zeros((B, ML_HEADS), f32)
        chunk_len = CHUNK
    else:
        chunk_len = T
    hm, c_new, n_new, m_new = mlstm_scan(mq.reshape(mshape), mk.reshape(mshape) * (ML_HEAD_DIM ** -0.5), mv.reshape(mshape), ig, lf, c0, n0, m0, chunk_len)
    hm = jax.nn.sigmoid(mo) * head_rmsnorm(hm, mlstm_norm_w).astype(x.dtype)
    q = rope(sq.reshape(B, T, SWA_HEADS, SWA_HEAD_DIM), pos)
    k = rope(sk.reshape(B, T, SWA_KV_HEADS, SWA_HEAD_DIM), pos)
    v = sv.reshape(B, T, SWA_KV_HEADS, SWA_HEAD_DIM)
    if prompt:
        hs = swa_prompt(q, k, v, swa_sinks)
        k_win = k[:, -WINDOW:]
        v_win = v[:, -WINDOW:]
    else:
        k_all = jnp.concatenate([k_cache.astype(k.dtype), k], axis=1)
        v_all = jnp.concatenate([v_cache.astype(v.dtype), v], axis=1)
        hs = swa_sample(q, k_all, v_all, swa_sinks)
        k_win = k_all[:, -WINDOW:]
        v_win = v_all[:, -WINDOW:]
    x = x + jnp.concatenate([hm, hs], axis=-1) @ w_out
    h2 = rmsnorm(x, norm_ffn_w)
    blocks = h2.reshape(B * T // PEER_BLOCK, PEER_BLOCK, D_MODEL) if prompt else h2
    x = x + peer(blocks, peer_w_q, peer_sub_keys_1, peer_sub_keys_2, peer_u, peer_v).reshape(B, T, D_MODEL)
    return x, k_win, v_win, c_new, n_new, m_new

def setup_inputs(seed: int = 0) -> dict:
    key = jax.random.key(seed)
    ks = jax.random.split(key, 24)
    f32 = jnp.float32

    def nrm(k, shape, scale):
        return scale * jax.random.normal(k, shape, f32)

    x_prompt = nrm(ks[0], (BATCH, SEQ, D_MODEL), 1.0)
    x_sample = nrm(ks[1], (DEC_BATCH, DEC_SEQ, D_MODEL), 1.0)
    cache_swa_k = nrm(ks[2], (DEPTH, DEC_BATCH, WINDOW, SWA_KV_HEADS, SWA_HEAD_DIM), 1.0)
    cache_swa_v = nrm(ks[3], (DEPTH, DEC_BATCH, WINDOW, SWA_KV_HEADS, SWA_HEAD_DIM), 1.0)
    state_mlstm_c = nrm(ks[4], (DEPTH, DEC_BATCH, ML_HEADS, ML_HEAD_DIM, ML_HEAD_DIM), 0.05)
    state_mlstm_n = nrm(ks[5], (DEPTH, DEC_BATCH, ML_HEADS, ML_HEAD_DIM), 0.1)
    state_mlstm_m = nrm(ks[6], (DEPTH, DEC_BATCH, ML_HEADS), 1.0)
    norm_mix_w = 1.0 + nrm(ks[7], (DEPTH, D_MODEL), 0.02)
    w_in = nrm(ks[8], (DEPTH, D_MODEL, IN_COLS), D_MODEL ** -0.5)
    i_bias = nrm(ks[9], (DEPTH, ML_HEADS), 0.1)
    f_bias = 3.0 + jnp.linspace(0.0, 3.0, ML_HEADS, dtype=f32) + nrm(ks[10], (DEPTH, ML_HEADS), 0.1)
    mlstm_if_bias = jnp.concatenate([i_bias, f_bias], axis=-1)
    mlstm_norm_w = 1.0 + nrm(ks[11], (DEPTH, ML_WIDTH), 0.02)
    swa_sinks = nrm(ks[12], (DEPTH, SWA_HEADS), 0.5)
    w_out = nrm(ks[13], (DEPTH, MIX_WIDTH, D_MODEL), MIX_WIDTH ** -0.5)
    norm_ffn_w = 1.0 + nrm(ks[14], (DEPTH, D_MODEL), 0.02)
    peer_w_q = nrm(ks[15], (DEPTH, D_MODEL, PEER_HEADS * PEER_KEY_DIM), D_MODEL ** -0.5)
    peer_sub_keys_1 = nrm(ks[16], (DEPTH, N_KEYS, PEER_HALF), PEER_HALF ** -0.5)
    peer_sub_keys_2 = nrm(ks[17], (DEPTH, N_KEYS, PEER_HALF), PEER_HALF ** -0.5)
    peer_u = nrm(ks[18], (DEPTH, N_EXPERTS, D_MODEL), D_MODEL ** -0.5)
    peer_v = nrm(ks[19], (DEPTH, N_EXPERTS, D_MODEL), 0.5)
    norm_final_w = 1.0 + nrm(ks[20], (D_MODEL,), 0.02)
    return {"x_prompt": x_prompt, "x_sample": x_sample,
            "cache_swa_k": cache_swa_k, "cache_swa_v": cache_swa_v,
            "state_mlstm_c": state_mlstm_c, "state_mlstm_n": state_mlstm_n, "state_mlstm_m": state_mlstm_m,
            "norm_mix_w": norm_mix_w, "w_in": w_in, "mlstm_if_bias": mlstm_if_bias, "mlstm_norm_w": mlstm_norm_w,
            "swa_sinks": swa_sinks, "w_out": w_out, "norm_ffn_w": norm_ffn_w,
            "peer_w_q": peer_w_q, "peer_sub_keys_1": peer_sub_keys_1, "peer_sub_keys_2": peer_sub_keys_2,
            "peer_u": peer_u, "peer_v": peer_v, "norm_final_w": norm_final_w}

def reference(x_prompt, x_sample, cache_swa_k, cache_swa_v, state_mlstm_c, state_mlstm_n, state_mlstm_m,
              norm_mix_w, w_in, mlstm_if_bias, mlstm_norm_w, swa_sinks, w_out, norm_ffn_w,
              peer_w_q, peer_sub_keys_1, peer_sub_keys_2, peer_u, peer_v, norm_final_w):
    pos_p = jnp.arange(x_prompt.shape[1], dtype=jnp.int32)
    pos_s = PAST_LEN + jnp.arange(x_sample.shape[1], dtype=jnp.int32)
    xp = x_prompt
    xs = x_sample
    kp_l, vp_l, cp_l, np_l, mp_l = [], [], [], [], []
    ks_l, vs_l, cs_l, ns_l, ms_l = [], [], [], [], []
    for l in range(DEPTH):
        w = (norm_mix_w[l], w_in[l], mlstm_if_bias[l], mlstm_norm_w[l], swa_sinks[l], w_out[l],
             norm_ffn_w[l], peer_w_q[l], peer_sub_keys_1[l], peer_sub_keys_2[l], peer_u[l], peer_v[l])
        xp, kp, vp, cp, npv, mp = layer(xp, pos_p, True, None, None, None, None, None, *w)
        xs, ksn, vsn, csn, nsn, msn = layer(xs, pos_s, False, cache_swa_k[l], cache_swa_v[l],
                                            state_mlstm_c[l], state_mlstm_n[l], state_mlstm_m[l], *w)
        kp_l.append(kp); vp_l.append(vp); cp_l.append(cp); np_l.append(npv); mp_l.append(mp)
        ks_l.append(ksn); vs_l.append(vsn); cs_l.append(csn); ns_l.append(nsn); ms_l.append(msn)
    y_prompt = rmsnorm(xp, norm_final_w)
    y_sample = rmsnorm(xs, norm_final_w)
    new_swa_k_prompt = jnp.stack(kp_l, axis=0)
    new_swa_v_prompt = jnp.stack(vp_l, axis=0)
    new_mlstm_c_prompt = jnp.stack(cp_l, axis=0)
    new_mlstm_n_prompt = jnp.stack(np_l, axis=0)
    new_mlstm_m_prompt = jnp.stack(mp_l, axis=0)
    new_swa_k_sample = jnp.stack(ks_l, axis=0)
    new_swa_v_sample = jnp.stack(vs_l, axis=0)
    new_mlstm_c_sample = jnp.stack(cs_l, axis=0)
    new_mlstm_n_sample = jnp.stack(ns_l, axis=0)
    new_mlstm_m_sample = jnp.stack(ms_l, axis=0)
    return (y_prompt, y_sample,
            new_swa_k_prompt, new_swa_v_prompt, new_mlstm_c_prompt, new_mlstm_n_prompt, new_mlstm_m_prompt,
            new_swa_k_sample, new_swa_v_sample, new_mlstm_c_sample, new_mlstm_n_sample, new_mlstm_m_sample)


_drawn_inputs = setup_inputs


def setup_inputs(seed=0):
    import zlib

    import numpy as np

    out = dict(_drawn_inputs(seed))
    spreads = {}
    factors = {'swa_sinks': 8.0, 'norm_final_w': 2.951}
    for name, (base, spread) in spreads.items():
        noise = np.random.default_rng([zlib.crc32(name.encode()), seed]).standard_normal(out[name].shape)
        drawn = base * np.exp(spread * noise) if base else spread * noise
        out[name] = jnp.asarray(drawn.astype(out[name].dtype))
    for name, factor in factors.items():
        out[name] = (out[name] * factor).astype(out[name].dtype)
    return out
```

```python
from contextlib import ExitStack

import concourse.bass as bass
import numpy as np
from concourse import mybir

F32 = mybir.dt.float32
U32 = mybir.dt.uint32
I32 = mybir.dt.int32
ALU = mybir.AluOpType
ACT = mybir.ActivationFunctionType
AX = mybir.AxisListType

P = 128
D = 1024
DC = D // P
SEQ = 1024
DEC = 32
PAST = 512
MH, MD = 4, 128
MW = MH * MD
QH, KVH, HD = 8, 2, 64
GRP = QH // KVH
WIN = 128
CHUNK = 64
ROT = 8
THETA = 500000.0
COLS = 4 * MW + 2 * MH + QH * HD + 2 * KVH * HD
OFF_Q, OFF_K, OFF_V, OFF_O = 0, MW, 2 * MW, 3 * MW
OFF_G = 4 * MW
OFF_SQ = OFF_G + 2 * MH
OFF_SK = OFF_SQ + QH * HD
OFF_SV = OFF_SK + KVH * HD
PH, NK, TOPK = 8, 128, 16
QC = 2 * PH
EPS = 1e-6
BIG = 1e30
LOW = -3.0e38
TILES = 1 + SEQ // P
NU = 4
NV = 4
STEPS = 39
LAST_SLOT = 90
PC = [(c, min(512, COLS - c)) for c in range(0, COLS, 512)]


def step_at(slot):
    return [s for s in range(STEPS) if s * LAST_SLOT // STEPS == slot]


def program(nc, x_prompt, x_sample, cache_k, cache_v, st_c, st_n, st_m, norm_mix_w, w_in, if_bias, mnorm_w, sinks,
            w_out, norm_ffn_w, w_q, keys_1, keys_2, peer_u, peer_v, norm_final_w, rot_tab,
            y, kp, vp, cp, np_, mp, ks, vs, cs, ns, ms):
    xp_d = x_prompt.rearrange("a s d -> (a s) d")
    xs_d = x_sample.rearrange("a s d -> (a s) d")
    u_d = peer_u.rearrange("a e d -> (a e) d")
    v_d = peer_v.rearrange("a e d -> (a e) d")
    proj_d = nc.dram_tensor("proj_scratch", (TILES * P, COLS), F32, kind="Internal").ap()

    with ExitStack() as ctx:
        def sb(name, shape, dt=F32):
            return ctx.enter_context(nc.sbuf_tensor(name, shape, dt))

        def sem(name):
            return ctx.enter_context(nc.semaphore(name))

        weights = sb("weights", [P, DC * 2 * PH * NK + DC * D])
        win_s = weights[:, 0:DC * COLS].rearrange("p (k c) -> p k c", k=DC)
        wq_s = weights[:, 0:DC * QC * NK].rearrange("p (k c) -> p k c", k=DC)
        wout_s = weights[:, DC * QC * NK:].rearrange("p (k c) -> p k c", k=DC)
        ring = sb("ring", [P, NU + NV, D])
        pj = sb("pj", [P, COLS])
        xt = sb("xt", [P, D])
        cat = sb("cat", [P, D])
        h2 = sb("h2", [P, D])
        reg = sb("reg", [P, 3588])
        qkT = reg[:, 0:1024].rearrange("p (h t) -> p h t", h=8)
        dT = reg[:, 1024:1536].rearrange("p (h t) -> p h t", h=MH)
        wT = reg[:, 1536:2048].rearrange("p (h t) -> p h t", h=MH)
        num = reg[:, 2048:2048 + MH * 129].rearrange("p (h e) -> p h e", h=MH)
        hm = reg[:, 2564:3076].rearrange("p (h e) -> p h e", h=MH)
        sq = reg[:, 3076:3588].rearrange("p (h e) -> p h e", h=MH)
        qr = reg[:, 0:512].rearrange("p (j g d) -> p j g d", j=GRP, g=KVH)
        qTs = reg[:, 512:1024].rearrange("p (j t) -> p j t", j=GRP)
        sm = reg[:, 1024:3072].rearrange("p (h s) -> p h s", h=QH)
        t8 = reg[:, 0:1024].rearrange("p (k t) -> p k t", k=DC)
        pT = pj[:, 0:2048].rearrange("p (h b t) -> p h b t", h=QH, b=2)
        qT = pj[:, 0:2048].rearrange("p (c t) -> p c t", c=QC)
        vx = sb("vx", [P, MH, 129])
        ct = sb("ct", [P, MH, 129])
        mb = sb("mb", [P, MH])
        mrow = sb("mrow", [MH, 1])
        ktw = sb("ktw", [P, 2 * P])
        vprev = sb("vprev", [P, P])
        kprev = sb("kprev", [P, P])
        sc = sb("sc", [P, QC, NK])
        rot = sb("rot", [P, 2 * ROT])
        rt = reg[:, 1024:1024 + 4 * (QH + KVH) * ROT].rearrange("p (i h r) -> p i h r", i=4, r=ROT)
        g8 = sb("g8", [P, 8])
        gab = sb("gab", [P, 3, MH])
        lf = sb("lf", [P, MH])
        acol = sb("acol", [P, MH])
        bsum = sb("bsum", [P, 8])
        rows = sb("rows", [MH, 3, P])
        ea = sb("ea", [P, 12])
        ex = sb("ex", [P, 12])
        d4 = sb("d4", [P, 5, MH])
        s8 = sb("s8", [P, 6, QH])
        nr = sb("nr", [P, 4])
        t2 = sb("t2", [P, 2, TOPK])
        i2 = sb("i2", [P, 2, TOPK], U32)
        i2f = sb("i2f", [P, 2, TOPK])
        cand = sb("cand", [P, TOPK, TOPK])
        top = sb("top", [P, 2, TOPK])
        sel = sb("sel", [P, TOPK], U32)
        ij = sb("ij", [P, 2, TOPK], U32)
        oh = sb("oh", [P, 2, TOPK, TOPK])
        r2 = sb("r2", [P, 2, TOPK])
        idx = sb("idx", [P, 4, TOPK], U32)
        ntop = sb("ntop", [P, 2])
        ew = sb("ew", [P, TOPK])
        ez = sb("ez", [P, 2])
        dots = sb("dots", [P, 2, TOPK])
        gl = sb("gl", [P, TOPK])
        coef = sb("coef", [P, 2, TOPK])
        diag = sb("diag", [P, NV, P])
        yo = sb("yo", [P, D])
        yr = sb("yr", [P, 3])
        ident = sb("ident", [P, P])
        triu = sb("triu", [P, P])
        ntriu = sb("ntriu", [P, P])
        dmask = sb("dmask", [P, P])
        ones = sb("ones", [P, P])
        wmask = sb("wmask", [P, 2, 2 * P])
        iota_i = sb("iota_i", [P, TOPK], I32)
        iota = sb("iota", [P, TOPK])
        bias8 = sb("bias8", [P, 8])
        sink8 = sb("sink8", [P, QH])
        mnw = sb("mnw", [P, MW])
        ffw = sb("ffw", [P, D])
        fiw = sb("fiw", [P, D])
        kT = sb("kT", [P, 2, NK])
        epsc = sb("epsc", [P, 1])
        x1 = [ring[:, b, :] for b in range(2)]
        h1 = [ring[:, 2 + b, :] for b in range(2)]
        hT1 = [ring[:, 4 + b, :].rearrange("p (k t) -> p k t", k=DC) for b in range(2)]
        nmw = ring[:, 6, :]
        po = [pj[:, :], reg[:, 0:COLS]]
        r1 = nr

        mx = ctx.enter_context(nc.psum_tensor("mx", [P, 4, 512], F32))
        h2p = ctx.enter_context(nc.psum_tensor("h2p", [P, D], F32))
        acc = ctx.enter_context(nc.psum_tensor("acc", [P, D], F32))
        pbank = [mx[:, 2, :], mx[:, 3, :], h2p[:, 0:512], h2p[:, 512:], acc[:, 0:512], acc[:, 512:]]
        bcol, blast = mx[:, 0, 0:4], mx[:, 0, 4:8]
        gcol, glast = mx[:, 0, 8:12], mx[:, 0, 12:16]
        brow, arow = mx[0:MH, 0, 16:144], mx[0:MH, 0, 144:272]

        const_in, pool_const, const_ready = sem("const_in"), sem("pool_const"), sem("const_ready")
        win_in, x1_in = sem("win_in"), [sem("x1_in0"), sem("x1_in1")]
        rms1_ready, h1_ready, h1_transposed = sem("rms1_ready"), sem("h1_ready"), sem("h1_transposed")
        hT1_act, hT1_dve, chunk_ready = sem("hT1_act"), sem("hT1_dve"), sem("chunk_ready")
        chunk_act, chunk_dve = sem("chunk_act"), sem("chunk_dve")
        proj_out, po_free = sem("proj_out"), sem("po_free")
        w2_in, keysT_ready, keysT_done = sem("w2_in"), sem("keysT_ready"), sem("keysT_done")
        state_in, stateT_ready, state_set = sem("state_in"), sem("stateT_ready"), sem("state_set")
        p_in, x_in = sem("p_in"), sem("x_in")
        gates_ready, softplus_ready, lf_ready = sem("gates_ready"), sem("softplus_ready"), sem("lf_ready")
        qk_transposed, mqT_ready, mkT_ready = sem("qk_transposed"), sem("mqT_ready"), sem("mkT_ready")
        sums_ready, qk_ready, grow_ready = sem("sums_ready"), sem("qk_ready"), sem("grow_ready")
        gb_ready, dT_ready, exparg_ready, ex_ready = sem("gb_ready"), sem("dT_ready"), sem("exparg_ready"), sem("ex_ready")
        wT_ready, num_ready, inter_ready = sem("wT_ready"), sem("num_ready"), sem("inter_ready")
        ssq_ready, dc_ready, state_ready, mrms_ready = sem("ssq_ready"), sem("dc_ready"), sem("state_ready"), sem("mrms_ready")
        rope_ready, qr_ready, swa_transposed = sem("rope_ready"), sem("qr_ready"), sem("swa_transposed")
        sqT_ready, skT_ready, swa_scored = sem("sqT_ready"), sem("skT_ready"), sem("swa_scored")
        smarg_ready, probs_ready, probs_transposed = sem("smarg_ready"), sem("probs_ready"), sem("probs_transposed")
        pT_act, pT_dve, attn_ready, cat_ready = sem("pT_act"), sem("pT_dve"), sem("attn_ready"), sem("cat_ready")
        rows_transposed, t8_act, t8_dve = sem("rows_transposed"), sem("t8_act"), sem("t8_dve")
        mixed_ready, x2_ready, rms2_ready, h2_ready = sem("mixed_ready"), sem("x2_ready"), sem("rms2_ready"), sem("h2_ready")
        query_ready, qT_ready, keys_scored, sc_ready = sem("query_ready"), sem("qT_ready"), sem("keys_scored"), sem("sc_ready")
        topk_done, pool_step, dve_step = sem("topk_done"), sem("pool_step"), sem("dve_step")
        u_in = [sem(f"u_in{i}") for i in range(NU)]
        v_in = [sem(f"v_in{i}") for i in range(NV)]
        u_free, v_free = sem("u_free"), sem("v_free")
        dots_done, gelu_ready, coef_ready, diag_ready = sem("dots_done"), sem("gelu_ready"), sem("coef_ready"), sem("diag_ready")
        acc_set, acc_done, yrms_ready, y_ready, y_out = sem("acc_set"), sem("acc_done"), sem("yrms_ready"), sem("y_ready"), sem("y_out")
        outs_done, st_ready, st_copied, st_out = sem("outs_done"), sem("st_ready"), sem("st_copied"), sem("st_out")

        def copy_probs(eng, half, n):
            copy = eng.copy if half == 0 else eng.tensor_copy
            src = mx[:, 2 * half:2 * half + 2, :].rearrange("p b (h w t) -> p (b h) w t", h=2, w=2)
            dst = pT[:, 4 * half:4 * half + 4, :, :]
            copy(dst[:, :, 0, 0:n], src[:, :, 0, 0:n])
            copy(dst[0:n, :, 1, 0:n], src[0:n, :, 1, 0:n])

        block = ctx.enter_context(nc.Block())

        @block.sync
        def _(sp):
            for dst, src in ((nmw, norm_mix_w[0]), (ffw[:, :], norm_ffn_w[0]), (fiw[:, :], norm_final_w),
                             (mnw[:, :], mnorm_w[0]), (bias8[:, :], if_bias[0]), (sink8[:, :], sinks[0])):
                sp.dma_start(dst, src.partition_broadcast(P)).then_inc(const_in, 16)
            sp.dma_start(cat[:, 0:P], keys_1[0]).then_inc(const_in, 16)
            sp.dma_start(cat[:, P:2 * P], keys_2[0]).then_inc(const_in, 16)

            def load_x1(m, b):
                if not isinstance(m, int) or m >= 2:
                    sp.wait_ge(h1_ready, m - 1)
                if isinstance(m, int) and m == 0:
                    sp.dma_start(x1[b][0:DEC, :], xs_d).then_inc(x1_in[b], 16)
                else:
                    sp.dma_start(x1[b], xp_d[bass.ds((m - 1) * P, P), :]).then_inc(x1_in[b], 16)

            def store_proj(m, b, n):
                sp.wait_ge(chunk_act, 3 * m + 3)
                sp.wait_ge(chunk_dve, 3 * m + 3)
                sp.dma_start(proj_d[bass.ds(m * P, n), :], po[b][0:n, :]).then_inc(proj_out, 16)
                sp.wait_ge(proj_out, 16 * (m + 1))
                sp.sem_inc(po_free, 1)

            sp.sem_inc(po_free, 2)
            load_x1(0, 0)
            load_x1(1, 1)
            for k in range(DC):
                sp.dma_start(win_s[:, k, :], w_in[0, k * P:(k + 1) * P, :]).then_inc(win_in, 16)
            load_x1(2, 0)
            store_proj(0, 0, DEC)
            with sp.Fori(0, TILES // 2 - 1) as j:
                load_x1(2 * j + 3, 1)
                store_proj(2 * j + 1, 1, P)
                load_x1(2 * j + 4, 0)
                store_proj(2 * j + 2, 0, P)
            store_proj(TILES - 2, 1, P)
            store_proj(TILES - 1, 0, P)

            sp.wait_ge(chunk_ready, 6 * TILES)
            sp.dma_start(wout_s, w_out[0].rearrange("(k p) c -> p k c", p=P)).then_inc(w2_in, 16)
            sp.dma_start(wq_s, w_q[0].rearrange("(k p) c -> p k c", p=P)).then_inc(w2_in, 16)
            sp.wait_ge(keysT_done, 1)
            sp.dma_start(cat[:, 0:MW].rearrange("e (h d) -> e h d", h=MH), st_c[0, 0].rearrange("h e d -> e h d")).then_inc(state_in, 16)
            sp.dma_start(cat[0:MH, 512:640], st_n[0, 0]).then_inc(state_in, 16)
            sp.dma_start(cat[:, 640:768], cache_k[0, 0].rearrange("s g d -> s (g d)")).then_inc(state_in, 16)
            sp.dma_start(vprev[:, :], cache_v[0, 0].rearrange("s g d -> s (g d)")).then_inc(state_in, 16)
            sp.dma_start(mb[:, :], st_m[0, 0].partition_broadcast(P)).then_inc(state_in, 16)
            sp.dma_start(mrow[:, :], st_m[0, 0].rearrange("(h a) -> h a", a=1)).then_inc(state_in, 16)

            def load_p(m, n):
                if not (isinstance(m, int) and m == 0):
                    sp.wait_ge(keys_scored, m)
                sp.dma_start(pj[0:n, :], proj_d[bass.ds(m * P, n), :]).then_inc(p_in, 16)
                sp.dma_start(rot[0:n, :], rot_tab[bass.ds(m * P, n), :]).then_inc(p_in, 16)

            def load_x(m):
                sp.wait_ge(acc_set, m)
                sp.dma_start(xt[:, :], xp_d[bass.ds((m - 1) * P, P), :]).then_inc(x_in, 16)

            def store_y(m):
                sp.wait_ge(y_ready, m + 1)
                sp.dma_start(y[bass.ds(m * P, P), :], yo[:, :]).then_inc(y_out, 16)

            def store_state(c, n_, m_, count):
                sp.wait_ge(st_copied, count)
                sp.dma_start(c[0, 0].rearrange("h e d -> e h d"), cat[:, 0:MW].rearrange("e (h d) -> e h d", h=MH)).then_inc(st_out, 16)
                sp.dma_start(n_[0, 0], cat[0:MH, 512:640]).then_inc(st_out, 16)
                sp.dma_start(m_[0, 0].rearrange("(h a) -> h a", a=1), mrow[:, :]).then_inc(st_out, 16)

            load_p(0, DEC)
            sp.wait_ge(const_ready, 1)
            sp.dma_start(xt[0:DEC, :], xs_d).then_inc(x_in, 16)
            for old, new in ((cache_k, ks), (cache_v, vs)):
                sp.dma_start(new[0, 0, 0:WIN - DEC], old[0, 0, DEC:WIN]).then_inc(outs_done, 16)
            sp.wait_ge(rope_ready, 1)
            sp.dma_start(ks[0, 0, WIN - DEC:WIN].rearrange("s g d -> s (g d)"), pj[0:DEC, OFF_SK:OFF_SV]).then_inc(outs_done, 16)
            sp.dma_start(vs[0, 0, WIN - DEC:WIN].rearrange("s g d -> s (g d)"), pj[0:DEC, OFF_SV:COLS]).then_inc(outs_done, 16)
            store_state(cs, ns, ms, 1)
            sp.wait_ge(outs_done, 16 * 4)
            load_p(1, P)
            load_x(1)
            with sp.Fori(0, TILES - 2) as j:
                load_p(j + 2, P)
                load_x(j + 2)
                store_y(j)
            store_state(cp, np_, mp, 2)
            sp.dma_start(kp[0, 0].rearrange("s g d -> s (g d)"), kprev[:, :]).then_inc(outs_done, 16)
            sp.dma_start(vp[0, 0].rearrange("s g d -> s (g d)"), vprev[:, :]).then_inc(outs_done, 16)
            store_y(TILES - 2)
            store_y(TILES - 1)
            sp.wait_ge(st_out, 16 * 6)
            sp.wait_ge(outs_done, 16 * 6)
            sp.wait_ge(y_out, 16 * TILES)

        @block.gpsimd
        def _(pool):
            for t, v in ((ident, 0.0), (triu, 1.0), (ntriu, -1.0), (dmask, 0.0), (ones, 1.0), (wmask, 0.0), (sc, 0.0),
                         (h2, 0.0), (dots, 0.0), (xt, 0.0), (ea, 0.0)):
                pool.memset(t[:], v)
            pool.iota(iota_i[:, :], [[1, TOPK]], base=0, channel_multiplier=0)
            pool.drain()
            pool.affine_select(out=ident[:, :], in_=ident[:, :], compare_op=ALU.not_equal, fill=1.0, base=0,
                               pattern=[[-1, P]], channel_multiplier=1)
            for t, fill in ((triu, 0.0), (ntriu, 0.0), (dmask, BIG)):
                pool.affine_select(out=t[:, :], in_=t[:, :], compare_op=ALU.is_ge, fill=fill, base=0,
                                   pattern=[[1, P]], channel_multiplier=-1)
            pool.drain()
            pool.memset(wmask[0:CHUNK, :, WIN + CHUNK:], -BIG)
            pool.drain()
            pool.memset(wmask[CHUNK:P, 1, 0:CHUNK], -BIG)
            pool.drain()
            pool.memset(wmask[:, 0, 0:WIN], -BIG)
            pool.drain().then_inc(pool_const, 1)
            pool.sem_inc(u_free, NU)
            pool.sem_inc(v_free, NV)

            def gather_u(g, h, k, n):
                if k == 0:
                    pool.wait_ge(topk_done, g + 1)
                pool.wait_ge(u_free, TOPK * g + k + 1)
                pool.sem_inc(pool_step, 1)
                pool.indirect_dma_start(ring[0:n, k % NU, :], None, u_d,
                                        bass.IndirectOffsetOnAxis(ap=idx[0:n, h % 4, k:k + 1], axis=0)).then_inc(u_in[k % NU], 16)

            def gather_v(g, h, k, n):
                pool.wait_ge(v_free, TOPK * g + k + 1)
                pool.sem_inc(pool_step, 1)
                pool.indirect_dma_start(ring[0:n, NU + k % NV, :], None, v_d,
                                        bass.IndirectOffsetOnAxis(ap=idx[0:n, h % 4, k:k + 1], axis=0)).then_inc(v_in[k % NV], 16)

            def tile(m, n, last):
                for h in range(PH):
                    for k in range(TOPK):
                        if h < PH - 1:
                            gather_u(PH * m + h + 1, h + 1, k, n)
                        elif not last:
                            gather_u(PH * (m + 1), 0, k, P)
                        gather_v(PH * m + h, h, k, n)

            for k in range(TOPK):
                gather_u(0, 0, k, DEC)
            tile(0, DEC, False)
            with pool.Fori(0, TILES - 2) as j:
                tile(j + 1, P, False)
            tile(TILES - 1, P, True)

        @block.scalar
        def _(act):
            S = nc.scalar

            def rms1(m, b, n, nth):
                act.wait_ge(x1_in[b], 16 * nth)
                if not (isinstance(m, int) and m == 0):
                    act.wait_ge(h1_ready, m)
                if not (isinstance(m, int) and m < 2):
                    act.wait_ge(chunk_ready, 6 * (m - 1))
                S.activation(hT1[b][0:n, :, :].rearrange("p k t -> p (k t)"), x1[b][0:n, :], ACT.Square, accum_out=nr[0:n, 0:1])
                act.drain()
                S.activation(nr[0:n, 1:2], nr[0:n, 0:1], ACT.Sqrt, scale=1.0 / D, bias=epsc[0:n, 0:1])
                act.drain().then_inc(rms1_ready, 1)

            def hT1_copy(m, b, n):
                act.wait_ge(h1_transposed, m + 1)
                S.copy(hT1[b][:, 0:4, 0:n], mx[:, 0, :].rearrange("p (k t) -> p k t", k=4)[:, :, 0:n])
                act.drain().then_inc(hT1_act, 1)

            def chunk_copy(m, b, n, c):
                act.wait_ge(chunk_ready, 6 * m + c + 1)
                act.wait_ge(po_free, m + 1)
                c0, w = PC[c]
                S.copy(po[b][0:n, c0:c0 + w], pbank[c][0:n, 0:w])
                act.drain().then_inc(chunk_act, 1)

            def proj_tile(m, b, n, nth, last=False):
                if not last:
                    rms1(m + 1, 1 - b, P, nth)
                chunk_copy(m, b, n, 0)
                chunk_copy(m, b, n, 2)
                if not last:
                    hT1_copy(m + 1, 1 - b, P)
                chunk_copy(m, b, n, 4)

            act.wait_ge(const_ready, 1)
            rms1(0, 0, DEC, 1)
            hT1_copy(0, 0, DEC)
            proj_tile(0, 0, DEC, 1)
            with act.Fori(0, TILES // 2 - 1) as j:
                proj_tile(2 * j + 1, 1, P, j + 2)
                proj_tile(2 * j + 2, 0, P, j + 2)
            proj_tile(TILES - 2, 1, P, TILES // 2 + 1)
            proj_tile(TILES - 1, 0, P, 0, last=True)

            def copy_state_out(count):
                act.wait_ge(st_ready, count)
                S.copy(cat[:, 0:MW], mx[:, 0, :])
                S.copy(cat[0:MH, 512:640], mx[0:MH, 1, 0:P])
                act.drain().then_inc(st_copied, 1)

            def mix(s, m, n):
                if s == 1:
                    act.wait_ge(gates_ready, m + 1)
                    S.activation(gab[0:n, 1, :], gab[0:n, 0, :], ACT.Exp, scale=-1.0)
                    act.drain()
                    S.activation(gab[0:n, 2, :], gab[0:n, 1, :], ACT.Ln, bias=ones[0:n, 0:1])
                    act.drain().then_inc(softplus_ready, 1)
                elif s == 2:
                    act.wait_ge(qk_transposed, m + 1)
                    S.copy(qkT[:, 0:4, 0:n], mx[:, 2, :].rearrange("p (h t) -> p h t", h=4)[:, :, 0:n])
                    act.drain().then_inc(mqT_ready, 1)
                elif s == 6:
                    act.wait_ge(gb_ready, m + 1)
                    for h in range(MH):
                        S.activation(dT[0:n, h, 0:n], mx[0:n, 1, h * P:h * P + n], ACT.Exp, scale=-1.0, bias=acol[0:n, h:h + 1])
                    act.drain().then_inc(dT_ready, 1)
                elif s == 7:
                    act.wait_ge(exparg_ready, m + 1)
                    S.activation(ex[:, :], ea[:, :], ACT.Exp)
                    act.drain().then_inc(ex_ready, 1)
                elif s == 9:
                    act.wait_ge(num_ready, m + 1)
                    for h in range(MH):
                        S.activation(num[0:n, h, :], mx[0:n, 2 + h // 2, h % 2 * 129:h % 2 * 129 + 129], ACT.Copy, scale=ex[0:n, h:h + 1])
                    act.drain().then_inc(inter_ready, 1)
                elif s == 11:
                    act.wait_ge(ssq_ready, m + 1)
                    S.activation(d4[0:n, 4, :], d4[0:n, 3, :], ACT.Sqrt, scale=1.0 / MD, bias=epsc[0:n, 0:1])
                    S.activation(pj[0:n, OFF_O:OFF_O + MW], pj[0:n, OFF_O:OFF_O + MW], ACT.Sigmoid)
                    act.drain().then_inc(mrms_ready, 1)
                elif s == 13:
                    act.wait_ge(rope_ready, m + 1)
                    S.copy(qr[0:n], pj[0:n, OFF_SQ:OFF_SK].rearrange("p (g j d) -> p j g d", g=KVH, j=GRP))
                    act.drain().then_inc(qr_ready, 1)
                elif s == 15:
                    act.wait_ge(swa_transposed, m + 1)
                    S.copy(qTs[:, :, 0:n], mx[:, 0, :].rearrange("p (j t) -> p j t", j=GRP)[:, :, 0:n])
                    act.drain().then_inc(sqT_ready, 1)
                elif s == 18:
                    act.wait_ge(smarg_ready, m + 1)
                    keys = WIN + n
                    for h in range(QH):
                        S.activation(sm[0:n, h, 0:keys], sm[0:n, h, 0:keys], ACT.Exp, bias=s8[0:n, 1, h:h + 1], accum_out=s8[0:n, 3, h:h + 1])
                    S.activation(s8[0:n, 4, :], s8[0:n, 2, :], ACT.Exp)
                    act.drain().then_inc(probs_ready, 1)
                elif s == 20:
                    act.wait_ge(probs_transposed, m + 1)
                    copy_probs(S, 0, n)
                    act.drain().then_inc(pT_act, 1)
                elif s in (24, 31):
                    second = int(s == 31)
                    act.wait_ge(rows_transposed, 2 * m + 1 + second)
                    S.copy(t8[:, 0:4, 0:n], mx[:, 0, :].rearrange("p (k t) -> p k t", k=4)[:, :, 0:n])
                    act.drain().then_inc(t8_act, 1)
                elif s == 28:
                    act.wait_ge(x2_ready, m + 1)
                    S.activation(cat[0:n, :], xt[0:n, :], ACT.Square, accum_out=nr[0:n, 0:1])
                    act.drain()
                    S.activation(nr[0:n, 1:2], nr[0:n, 0:1], ACT.Sqrt, scale=1.0 / D, bias=epsc[0:n, 0:1])
                    act.drain().then_inc(rms2_ready, 1)
                elif 33 <= s <= 36:
                    g = s - 33
                    act.wait_ge(query_ready, 4 * m + g + 1)
                    S.copy(qT[:, 4 * g:4 * g + 4, 0:n], mx[:, g, :].rearrange("p (c t) -> p c t", c=4)[:, :, 0:n])
                    act.drain().then_inc(qT_ready, 1)
                elif s == 38:
                    act.wait_ge(keys_scored, m + 1)
                    if not (isinstance(m, int) and m == 0):
                        act.wait_ge(topk_done, PH * m)
                    S.copy(sc[0:n, :, :].rearrange("p c k -> p (c k)"), mx[0:n, :, :].rearrange("p b c -> p (b c)"))
                    act.drain().then_inc(sc_ready, 1)

            def tile(m, n, nxt):
                for h in range(PH):
                    g = PH * m + h
                    act.wait_ge(dots_done, g + 1)
                    act.wait_ge(topk_done, g + 1)
                    S.activation(ew[:, :], top[:, h % 2, :], ACT.Exp, bias=ntop[:, h % 2:h % 2 + 1], accum_out=ez[:, 0:1])
                    S.activation(gl[:, :], dots[:, h % 2, :], ACT.Gelu)
                    act.drain().then_inc(gelu_ready, 1)
                    for k in range(TOPK):
                        if k == 0:
                            act.wait_ge(coef_ready, g + 1)
                        act.wait_ge(v_free, TOPK * g + k + 1)
                        S.activation(diag[:, k % NV, :], ident[:, :], ACT.Copy, scale=coef[:, h % 2, k:k + 1])
                        act.drain().then_inc(diag_ready, 1)
                        if nxt:
                            for s in step_at(TOPK * h + k):
                                mix(s, *nxt)
                act.wait_ge(acc_done, m + 1)
                if not (isinstance(m, int) and m == 0):
                    act.wait_ge(y_out, 16 * m)
                S.activation(yo[:, :], acc[:, :], ACT.Square, accum_out=yr[:, 0:1])
                act.drain()
                S.activation(yr[:, 1:2], yr[:, 0:1], ACT.Sqrt, scale=1.0 / D, bias=epsc[:, 0:1])
                act.drain().then_inc(yrms_ready, 1)

            for s in range(STEPS):
                mix(s, 0, DEC)
            copy_state_out(1)
            tile(0, DEC, (1, P))
            with act.Fori(0, TILES - 2) as j:
                tile(j + 1, P, (j + 2, P))
            copy_state_out(2)
            tile(TILES - 1, P, None)

        @block.vector
        def _(dve):
            V = nc.vector

            def bc(ap, *shape):
                return ap.broadcast_to(list(shape))

            dve.wait_ge(pool_const, 1)
            dve.wait_ge(const_in, 16 * 8)
            V.tensor_copy(iota[:, :], iota_i[:, :])
            V.memset(vx[:, :, 128:129], 1.0)
            V.memset(epsc[:, :], EPS)
            dve.drain().then_inc(const_ready, 1)

            def norm1(m, b, n):
                dve.wait_ge(rms1_ready, m + 1)
                V.reciprocal(nr[0:n, 2:3], nr[0:n, 1:2])
                dve.drain()
                V.scalar_tensor_tensor(h1[b][0:n, :], x1[b][0:n, :], nr[0:n, 2:3], nmw[0:n, :], ALU.mult, ALU.mult)
                dve.drain().then_inc(h1_ready, 1)

            def hT1_copy(m, b, n):
                dve.wait_ge(h1_transposed, m + 1)
                V.tensor_copy(hT1[b][:, 4:8, 0:n], mx[:, 1, :].rearrange("p (k t) -> p k t", k=4)[:, :, 0:n])
                dve.drain().then_inc(hT1_dve, 1)

            def chunk_copy(m, b, n, c):
                dve.wait_ge(chunk_ready, 6 * m + c + 1)
                dve.wait_ge(po_free, m + 1)
                c0, w = PC[c]
                V.tensor_copy(po[b][0:n, c0:c0 + w], pbank[c][0:n, 0:w])
                dve.drain().then_inc(chunk_dve, 1)

            def proj_tile(m, b, n, last=False):
                if not last:
                    norm1(m + 1, 1 - b, P)
                chunk_copy(m, b, n, 1)
                if not last:
                    hT1_copy(m + 1, 1 - b, P)
                chunk_copy(m, b, n, 3)
                chunk_copy(m, b, n, 5)

            norm1(0, 0, DEC)
            hT1_copy(0, 0, DEC)
            proj_tile(0, 0, DEC)
            with dve.Fori(0, TILES // 2 - 1) as j:
                proj_tile(2 * j + 1, 1, P)
                proj_tile(2 * j + 2, 0, P)
            proj_tile(TILES - 2, 1, P)
            proj_tile(TILES - 1, 0, P, last=True)

            dve.wait_ge(keysT_ready, 1)
            V.tensor_copy(kT[:, :, :].rearrange("p a k -> p (a k)"), mx[:, 0, 0:2 * NK])
            dve.drain().then_inc(keysT_done, 1)
            dve.wait_ge(stateT_ready, 1)
            V.tensor_copy(ct[:, :, 0:MD], mx[:, 0, :].rearrange("p (h e) -> p h e", h=MH))
            V.tensor_copy(ct[:, :, MD:MD + 1], mx[:, 1, 0:MH].rearrange("p (h a) -> p h a", a=1))
            V.tensor_copy(ktw[:, 0:P], mx[:, 2, 0:P])
            dve.drain().then_inc(state_set, 1)

            def mix(s, m, n):
                if s == 0:
                    dve.wait_ge(p_in, 32 * (m + 1))
                    V.tensor_tensor(g8[0:n, :], pj[0:n, OFF_G:OFF_SQ], bias8[0:n, :], ALU.add)
                    V.tensor_scalar(pj[0:n, OFF_K:OFF_V], pj[0:n, OFF_K:OFF_V], MD ** -0.5, None, ALU.mult)
                    V.tensor_copy(vx[0:n, :, 0:MD], pj[0:n, OFF_V:OFF_O].rearrange("p (h e) -> p h e", h=MH))
                    dve.drain()
                    V.scalar_tensor_tensor(gab[0:n, 0, :], g8[0:n, 4:8], -1.0, g8[0:n, 4:8], ALU.mult, ALU.max)
                    dve.drain().then_inc(gates_ready, 1)
                elif s == 2:
                    dve.wait_ge(softplus_ready, m + 1)
                    V.scalar_tensor_tensor(lf[0:n, :], g8[0:n, 4:8], 0.0, gab[0:n, 2, :], ALU.min, ALU.subtract)
                    dve.drain().then_inc(lf_ready, 1)
                    dve.wait_ge(qk_transposed, m + 1)
                    V.tensor_copy(qkT[:, 4:8, 0:n], mx[:, 3, :].rearrange("p (h t) -> p h t", h=4)[:, :, 0:n])
                    dve.drain().then_inc(mkT_ready, 1)
                elif s == 4:
                    dve.wait_ge(sums_ready, m + 1)
                    V.tensor_copy(bsum[0:n, 0:4], bcol[0:n, :])
                    V.tensor_copy(bsum[:, 4:8], blast)
                    V.tensor_copy(rows[:, 0, 0:n], brow[:, 0:n])
                    V.tensor_copy(rows[:, 1, 0:n], arow[:, 0:n])
                    dve.drain()
                    V.tensor_tensor(acol[0:n, :], g8[0:n, 0:4], bsum[0:n, 0:4], ALU.subtract)
                    V.tensor_tensor_scan(rows[:, 2, 0:n], rows[:, 1, 0:n], rows[:, 1, 0:n], mrow[:, :], ALU.max, ALU.max)
                    dve.drain()
                    V.tensor_tensor(mrow[:, :], rows[:, 0, n - 1:n], rows[:, 2, n - 1:n], ALU.add)
                    dve.drain().then_inc(grow_ready, 1)
                elif s == 6:
                    dve.wait_ge(gb_ready, m + 1)
                    V.tensor_tensor(ea[0:n, 0:4], mb[0:n, :], gcol[0:n, :], ALU.subtract)
                    V.scalar_tensor_tensor(ea[0:n, 4:8], gcol[0:n, :], -1.0, bsum[0:n, 0:4], ALU.mult, ALU.subtract)
                    V.tensor_tensor(ea[:, 8:12], mb[:, :], glast, ALU.subtract)
                    dve.drain()
                    V.tensor_tensor(mb[:, :], bsum[:, 4:8], glast, ALU.add)
                    dve.drain().then_inc(exparg_ready, 1)
                elif s == 7:
                    dve.wait_ge(dT_ready, m + 1)
                    dve.wait_ge(qk_ready, m + 1)
                    V.tensor_tensor(wT[0:n, :, 0:n], mx[0:n, 2, :].rearrange("p (h t) -> p h t", h=MH)[:, :, 0:n], dT[0:n, :, 0:n], ALU.mult)
                    pk = pj[0:n, OFF_K:OFF_V].rearrange("p (h d) -> p h d", h=MH)
                    V.tensor_tensor(pk, pk, bc(dT[0:n, :, n - 1:n], n, MH, MD), ALU.mult)
                    dve.drain().then_inc(wT_ready, 1)
                elif s == 10:
                    dve.wait_ge(inter_ready, m + 1)
                    dve.wait_ge(ex_ready, m + 1)
                    pair = num[0:n, :, :].rearrange("p (b h) e -> p b (h e)", b=2)
                    V.tensor_tensor(pair, pair, mx[0:n, 0:2, 0:258], ALU.add)
                    dve.drain()
                    den = num[0:n, :, MD:MD + 1].rearrange("p h a -> p (h a)")
                    V.scalar_tensor_tensor(d4[0:n, 0, :], den, -1.0, den, ALU.mult, ALU.max)
                    dve.drain()
                    V.tensor_tensor(d4[0:n, 1, :], d4[0:n, 0, :], ex[0:n, 4:8], ALU.max)
                    dve.drain()
                    V.reciprocal(d4[0:n, 2, :], d4[0:n, 1, :])
                    dve.drain()
                    V.tensor_tensor(hm[0:n, :, :], num[0:n, :, 0:MD], bc(d4[0:n, 2, :].unsqueeze(2), n, MH, MD), ALU.mult)
                    dve.drain()
                    V.tensor_tensor(sq[0:n, :, :], hm[0:n, :, :], hm[0:n, :, :], ALU.mult)
                    dve.drain()
                    V.tensor_reduce(d4[0:n, 3, :], sq[0:n, :, :], AX.X, ALU.add)
                    dve.drain().then_inc(ssq_ready, 1)
                elif s == 11:
                    dve.wait_ge(dc_ready, m + 1)
                    for h in range(MH):
                        V.scalar_tensor_tensor(ct[:, h, :], ct[:, h, :], ex[:, 8 + h:9 + h], mx[:, 2 + h // 2, h % 2 * 129:h % 2 * 129 + 129], ALU.mult, ALU.add)
                    dve.drain().then_inc(state_ready, 1)
                elif s == 12:
                    dve.wait_ge(mrms_ready, m + 1)
                    V.reciprocal(d4[0:n, 0, :], d4[0:n, 4, :])
                    qk = pj[0:n, OFF_SQ:OFF_SV].rearrange("p (h d) -> p h d", d=HD)
                    xa, xb = qk[:, :, 0:ROT], qk[:, :, ROT:2 * ROT]
                    cos = bc(rot[0:n, 0:ROT].unsqueeze(1), n, QH + KVH, ROT)
                    sin = bc(rot[0:n, ROT:2 * ROT].unsqueeze(1), n, QH + KVH, ROT)
                    for i, (a, b) in enumerate(((xa, cos), (xb, sin), (xb, cos), (xa, sin))):
                        V.tensor_tensor(rt[0:n, i], a, b, ALU.mult)
                    dve.drain()
                    V.tensor_tensor(xa, rt[0:n, 0], rt[0:n, 1], ALU.subtract)
                    V.tensor_tensor(xb, rt[0:n, 2], rt[0:n, 3], ALU.add)
                    V.tensor_tensor(sq[0:n, :, :], hm[0:n, :, :], bc(d4[0:n, 0, :].unsqueeze(2), n, MH, MD), ALU.mult)
                    dve.drain().then_inc(rope_ready, 1)
                    V.tensor_tensor(hm[0:n, :, :].rearrange("p h e -> p (h e)"), sq[0:n, :, :].rearrange("p h e -> p (h e)"), mnw[0:n, :], ALU.mult)
                    dve.drain()
                    V.tensor_tensor(cat[0:n, 0:MW], hm[0:n, :, :].rearrange("p h e -> p (h e)"), pj[0:n, OFF_O:OFF_O + MW], ALU.mult)
                elif s == 15:
                    dve.wait_ge(swa_transposed, m + 1)
                    V.tensor_copy(ktw[:, WIN:WIN + n], mx[:, 1, 0:n])
                    dve.drain().then_inc(skT_ready, 1)
                elif s == 17:
                    dve.wait_ge(swa_scored, m + 1)
                    keys = WIN + n
                    scores = mx[0:n, :, :].rearrange("p b (h s) -> p (b h) s", h=2)[:, :, 0:keys]
                    if n == P:
                        V.scalar_tensor_tensor(sm[0:n, :, 0:keys], scores, HD ** -0.5, bc(wmask[0:n, 0:1, 0:keys], n, QH, keys), ALU.mult, ALU.add)
                    else:
                        V.tensor_scalar(sm[0:n, :, 0:keys], scores, HD ** -0.5, None, ALU.mult)
                    dve.drain()
                    V.tensor_reduce(s8[0:n, 0, :], sm[0:n, :, 0:keys], AX.X, ALU.max)
                    dve.drain()
                    V.tensor_tensor(s8[0:n, 5, :], s8[0:n, 0, :], sink8[0:n, :], ALU.max)
                    dve.drain()
                    V.tensor_scalar(s8[0:n, 1, :], s8[0:n, 5, :], -1.0, None, ALU.mult)
                    V.tensor_tensor(s8[0:n, 2, :], sink8[0:n, :], s8[0:n, 5, :], ALU.subtract)
                    dve.drain().then_inc(smarg_ready, 1)
                elif s == 19:
                    dve.wait_ge(probs_ready, m + 1)
                    V.tensor_tensor(s8[0:n, 0, :], s8[0:n, 3, :], s8[0:n, 4, :], ALU.add)
                    dve.drain()
                    V.reciprocal(s8[0:n, 5, :], s8[0:n, 0, :])
                elif s == 20:
                    dve.wait_ge(probs_transposed, m + 1)
                    copy_probs(V, 1, n)
                    dve.drain().then_inc(pT_dve, 1)
                elif s == 22:
                    dve.wait_ge(attn_ready, m + 1)
                    V.tensor_tensor(cat[0:n, MW:D].rearrange("p (h d) -> p h d", h=QH), mx[0:n, 0, :].rearrange("p (h d) -> p h d", h=QH),
                                    bc(s8[0:n, 5, :].unsqueeze(2), n, QH, HD), ALU.mult)
                    if n == P:
                        V.tensor_copy(ktw[:, 0:WIN], ktw[:, WIN:2 * WIN])
                        V.tensor_copy(vprev[:, :], pj[:, OFF_SV:COLS])
                        V.tensor_copy(kprev[:, :], pj[:, OFF_SK:OFF_SV])
                        V.tensor_copy(wmask[:, 0, :], wmask[:, 1, :])
                    dve.drain().then_inc(cat_ready, 1)
                elif s in (24, 31):
                    second = int(s == 31)
                    dve.wait_ge(rows_transposed, 2 * m + 1 + second)
                    V.tensor_copy(t8[:, 4:8, 0:n], mx[:, 1, :].rearrange("p (k t) -> p k t", k=4)[:, :, 0:n])
                    dve.drain().then_inc(t8_dve, 1)
                elif s == 27:
                    dve.wait_ge(mixed_ready, m + 1)
                    dve.wait_ge(x_in, 16 * (m + 1))
                    V.tensor_tensor(xt[0:n, :], xt[0:n, :], mx[0:n, 2:4, :].rearrange("p b c -> p (b c)"), ALU.add)
                    dve.drain().then_inc(x2_ready, 1)
                elif s == 29:
                    dve.wait_ge(rms2_ready, m + 1)
                    V.reciprocal(nr[0:n, 2:3], nr[0:n, 1:2])
                    dve.drain()
                    V.scalar_tensor_tensor(h2[0:n, :], xt[0:n, :], nr[0:n, 2:3], ffw[0:n, :], ALU.mult, ALU.mult)
                    dve.drain().then_inc(h2_ready, 1)

            def topk(g, h, part, m=None):
                s1, s2 = sc[:, 2 * h, :], sc[:, 2 * h + 1, :]
                cd = cand[:, :, :].rearrange("p a b -> p (a b)")
                tp = top[:, h % 2, :]
                dve.drain()
                if part == 0:
                    if m is not None:
                        dve.wait_ge(sc_ready, m + 1)
                        dve.sem_inc(dve_step, 1)
                    V.max(t2[:, 0, 0:8], s1)
                    V.max(t2[:, 1, 0:8], s2)
                    dve.drain()
                    V.max_index(i2[:, 0, 0:8], t2[:, 0, 0:8], s1)
                    V.max_index(i2[:, 1, 0:8], t2[:, 1, 0:8], s2)
                elif part == 1:
                    V.match_replace(s1, t2[:, 0, 0:8], s1, LOW)
                    V.match_replace(s2, t2[:, 1, 0:8], s2, LOW)
                    dve.drain()
                    V.max(t2[:, 0, 8:16], s1)
                    V.max(t2[:, 1, 8:16], s2)
                elif part == 2:
                    V.max_index(i2[:, 0, 8:16], t2[:, 0, 8:16], s1)
                    V.max_index(i2[:, 1, 8:16], t2[:, 1, 8:16], s2)
                    V.tensor_tensor(cand[:, :, :], bc(t2[:, 0, :].unsqueeze(2), P, TOPK, TOPK), bc(t2[:, 1, :].unsqueeze(1), P, TOPK, TOPK), ALU.add)
                    dve.drain()
                    V.tensor_copy(i2f[:, :, :], i2[:, :, :])
                elif part == 3:
                    V.max(tp[:, 0:8], cd)
                elif part == 4:
                    V.max_index(sel[:, 0:8], tp[:, 0:8], cd)
                    V.tensor_scalar(ntop[:, h % 2:h % 2 + 1], tp[:, 0:1], -1.0, None, ALU.mult)
                elif part == 5:
                    V.match_replace(cd, tp[:, 0:8], cd, LOW)
                elif part == 6:
                    V.max(tp[:, 8:16], cd)
                elif part == 7:
                    V.max_index(sel[:, 8:16], tp[:, 8:16], cd)
                elif part == 8:
                    V.tensor_scalar(ij[:, 0, :], sel[:, :], 4, None, ALU.logical_shift_right)
                    V.tensor_scalar(ij[:, 1, :], sel[:, :], 15, None, ALU.bitwise_and)
                    dve.drain()
                    for a in range(2):
                        V.tensor_tensor(oh[:, a], bc(ij[:, a, :].unsqueeze(2), P, TOPK, TOPK), bc(iota[:, :].unsqueeze(1), P, TOPK, TOPK), ALU.is_equal)
                elif part == 9:
                    for a in range(2):
                        V.tensor_tensor(oh[:, a], oh[:, a], bc(i2f[:, a, :].unsqueeze(1), P, TOPK, TOPK), ALU.mult)
                    dve.drain()
                    V.tensor_reduce(r2[:, :, :], oh[:, :, :, :], AX.X, ALU.add)
                elif part == 10:
                    V.scalar_tensor_tensor(idx[:, h % 4, :], r2[:, 0, :], float(NK), r2[:, 1, :], ALU.mult, ALU.add)
                    dve.drain().then_inc(topk_done, 1)

            def weigh(g, h):
                dve.wait_ge(gelu_ready, g + 1)
                V.reciprocal(ez[:, 1:2], ez[:, 0:1])
                dve.drain()
                V.scalar_tensor_tensor(coef[:, h % 2, :], gl[:, :], ez[:, 1:2], ew[:, :], ALU.mult, ALU.mult)
                dve.drain().then_inc(coef_ready, 1)

            def finish(m):
                dve.wait_ge(yrms_ready, m + 1)
                V.reciprocal(yr[:, 2:3], yr[:, 1:2])
                dve.drain()
                V.scalar_tensor_tensor(yo[:, :], acc[:, :], yr[:, 2:3], fiw[:, :], ALU.mult, ALU.mult)
                dve.drain().then_inc(y_ready, 1)

            def tile(m, n, nxt):
                first = isinstance(m, int) and m == 0
                dve.drain()
                V.tensor_copy(h2p[:, :], h2[:, :])
                dve.drain()
                for h in range(PH):
                    g = PH * m + h
                    for k in range(TOPK):
                        dve.wait_ge(u_in[k % NU], 16 * (TOPK // NU * g + k // NU + 1))
                        V.scalar_tensor_tensor(ring[0:n, k % NU, :], ring[0:n, k % NU, :], 1.0, h2p[0:n, :], ALU.mult, ALU.mult,
                                               accum_out=dots[0:n, h % 2, k:k + 1]).then_inc(u_free, 1)
                        if k == TOPK - 1:
                            dve.drain().then_inc(dots_done, 1)
                        if k == 1 and not (first and h == 0):
                            weigh(g - 1, (h - 1) % PH)
                        if k == 2 and h == 1 and not first:
                            finish(m - 1)
                        if k <= 10 and h < PH - 1:
                            topk(g + 1, h + 1, k)
                        elif k <= 10 and nxt:
                            topk(g + 1, 0, k, m + 1)
                        slot = TOPK * (h - 1) + k
                        if nxt and slot >= 0:
                            for s in step_at(slot):
                                mix(s, *nxt)

            for s in range(STEPS):
                mix(s, 0, DEC)
            for part in range(11):
                topk(0, 0, part, 0)
            dve.wait_ge(st_out, 16 * 3)
            for t in (ct[:, :, :], mb[:, :], mrow[:, :], ktw[:, 0:WIN], vprev[:, :]):
                V.memset(t, 0.0)
            dve.drain()
            V.memset(vx[:, :, 128:129], 1.0)
            tile(0, DEC, (1, P))
            with dve.Fori(0, TILES - 2) as j:
                tile(j + 1, P, (j + 2, P))
            tile(TILES - 1, P, None)
            weigh(PH * TILES - 1, PH - 1)
            finish(TILES - 1)

        @block.tensor
        def _(pe):
            T = nc.tensor

            def transpose1(m, b, n):
                pe.wait_ge(h1_ready, m + 1)
                if not (isinstance(m, int) and m == 0):
                    pe.wait_ge(hT1_act, m)
                    pe.wait_ge(hT1_dve, m)
                for k in range(DC):
                    last = T.transpose(mx[:, k // 4, k % 4 * P:k % 4 * P + n], h1[b][0:n, k * P:(k + 1) * P], ident[0:n, 0:n])
                last.then_inc(h1_transposed, 1)

            def project(m, b, n, c):
                if c == 0:
                    pe.wait_ge(hT1_act, m + 1)
                    pe.wait_ge(hT1_dve, m + 1)
                if not (isinstance(m, int) and m == 0):
                    pe.wait_ge(chunk_dve if c % 2 else chunk_act, 3 * m - 3 + c // 2 + 1)
                c0, w = PC[c]
                for k in range(DC):
                    last = T.matmul(pbank[c][0:n, 0:w], hT1[b][:, k, 0:n], win_s[:, k, c0:c0 + w], start=k == 0, stop=k == DC - 1)
                last.then_inc(chunk_ready, 1)

            def proj_tile(m, b, n, last=False):
                for c in range(3):
                    project(m, b, n, c)
                if not last:
                    transpose1(m + 1, 1 - b, P)
                for c in range(3, 6):
                    project(m, b, n, c)

            pe.wait_ge(const_ready, 1)
            transpose1(0, 0, DEC)
            pe.wait_ge(win_in, 16 * DC)
            proj_tile(0, 0, DEC)
            with pe.Fori(0, TILES // 2 - 1) as j:
                proj_tile(2 * j + 1, 1, P)
                proj_tile(2 * j + 2, 0, P)
            proj_tile(TILES - 2, 1, P)
            proj_tile(TILES - 1, 0, P, last=True)

            for a in range(2):
                last = T.transpose(mx[:, 0, a * NK:(a + 1) * NK], cat[:, a * P:(a + 1) * P], ident[:, :])
            last.then_inc(keysT_ready, 1)
            pe.wait_ge(keysT_done, 1)
            pe.wait_ge(state_in, 16 * 6)
            for h in range(MH):
                T.transpose(mx[:, 0, h * P:(h + 1) * P], cat[:, h * P:(h + 1) * P], ident[:, :])
            T.transpose(mx[:, 1, 0:MH], cat[0:MH, 512:640], ident[0:MH, 0:MH])
            T.transpose(mx[:, 2, 0:P], cat[:, 640:768], ident[:, :]).then_inc(stateT_ready, 1)
            pe.wait_ge(state_set, 1)

            def store_state(count):
                pe.wait_ge(state_ready, 1 if count == 1 else TILES)
                pe.wait_ge(sc_ready, 1 if count == 1 else TILES)
                for h in range(MH):
                    T.transpose(mx[:, 0, h * P:(h + 1) * P], ct[:, h, 0:MD], ident[:, :])
                T.transpose(mx[0:MH, 1, 0:P], ct[:, :, MD:MD + 1].rearrange("p h a -> p (h a)"), ident[:, :]).then_inc(st_ready, 1)

            def mix(s, m, n):
                if s == 1:
                    pe.wait_ge(gates_ready, m + 1)
                    if not (isinstance(m, int) and m == 0):
                        pe.wait_ge(sc_ready, m)
                    if isinstance(m, int) and m == 1:
                        pe.wait_ge(st_copied, 1)
                    for a, off in ((0, OFF_Q), (1, OFF_K)):
                        for h in range(MH):
                            last = T.transpose(mx[:, 2 + a, h * P:h * P + n], pj[0:n, off + h * MD:off + (h + 1) * MD], ident[0:n, 0:n])
                    last.then_inc(qk_transposed, 1)
                elif s == 3:
                    pe.wait_ge(lf_ready, m + 1)
                    T.matmul(bcol[0:n, :], triu[0:n, 0:n], lf[0:n, :], start=True, stop=True)
                    T.matmul(blast, ones[0:n, :], lf[0:n, :], start=True, stop=True)
                    T.matmul(brow[:, 0:n], lf[0:n, :], triu[0:n, 0:n], start=True, stop=True)
                    T.matmul(arow[:, 0:n], lf[0:n, :], ntriu[0:n, 0:n], start=True, stop=False)
                    T.matmul(arow[:, 0:n], g8[0:n, 0:4], ident[0:n, 0:n], start=False, stop=True).then_inc(sums_ready, 1)
                    pe.wait_ge(mqT_ready, m + 1)
                    pe.wait_ge(mkT_ready, m + 1)
                    for h in range(MH):
                        last = T.matmul(mx[0:n, 2, h * P:h * P + n], qkT[:, 4 + h, 0:n], qkT[:, h, 0:n], start=True, stop=True)
                    last.then_inc(qk_ready, 1)
                elif s == 5:
                    pe.wait_ge(grow_ready, m + 1)
                    gb = mx[0:n, 1, :].rearrange("p (h t) -> p h t", h=MH)[:, :, 0:n]
                    T.matmul(gb, ident[0:n, 0:n], dmask[0:n, 0:n].unsqueeze(1).broadcast_to([n, MH, n]), start=True, stop=False)
                    for h in range(MH):
                        T.matmul(gb[:, h, :], ident[0:MH, h:h + 1].broadcast_to([MH, n]), rows[:, 2, 0:n], start=False, stop=h == MH - 1)
                    T.matmul(gcol[0:n, :], rows[:, 2, 0:n], ident[0:MH, 0:MH], start=True, stop=True)
                    for h in range(MH):
                        last = T.matmul(glast[:, h:h + 1], ident[0:MH, h:h + 1].broadcast_to([MH, P]), rows[:, 2, n - 1:n], start=True, stop=True)
                    last.then_inc(gb_ready, 1)
                elif s == 8:
                    pe.wait_ge(wT_ready, m + 1)
                    pe.wait_ge(exparg_ready, m + 1)
                    for h in range(MH):
                        T.matmul(mx[0:n, h // 2, h % 2 * 129:h % 2 * 129 + 129], wT[0:n, h, 0:n], vx[0:n, h, :], start=True, stop=True)
                    for h in range(MH):
                        last = T.matmul(mx[0:n, 2 + h // 2, h % 2 * 129:h % 2 * 129 + 129], qkT[:, h, 0:n], ct[:, h, :], start=True, stop=True)
                    last.then_inc(num_ready, 1)
                elif s == 10:
                    pe.wait_ge(inter_ready, m + 1)
                    for h in range(MH):
                        last = T.matmul(mx[:, 2 + h // 2, h % 2 * 129:h % 2 * 129 + 129], pj[0:n, OFF_K + h * MD:OFF_K + (h + 1) * MD], vx[0:n, h, :], start=True, stop=True)
                    last.then_inc(dc_ready, 1)
                elif s == 14:
                    pe.wait_ge(qr_ready, m + 1)
                    for j in range(GRP):
                        T.transpose(mx[:, 0, j * P:j * P + n], qr[0:n, j, :, :].rearrange("p g d -> p (g d)"), ident[0:n, 0:n])
                    T.transpose(mx[:, 1, 0:n], pj[0:n, OFF_SK:OFF_SV], ident[0:n, 0:n]).then_inc(swa_transposed, 1)
                elif s == 16:
                    pe.wait_ge(sqT_ready, m + 1)
                    pe.wait_ge(skT_ready, m + 1)
                    pe.wait_ge(state_ready, m + 1)
                    for h in range(QH):
                        r = slice(h // GRP * HD, h // GRP * HD + HD)
                        last = T.matmul(mx[0:n, h // 2, h % 2 * 256:h % 2 * 256 + WIN + n], qTs[r, h % GRP, 0:n], ktw[r, 0:WIN + n], start=True, stop=True)
                    last.then_inc(swa_scored, 1)
                elif s == 19:
                    pe.wait_ge(probs_ready, m + 1)
                    for h in range(QH):
                        c = h % 2 * 256
                        T.transpose(mx[:, h // 2, c:c + n], sm[0:n, h, 0:WIN], ident[0:n, 0:n])
                        last = T.transpose(mx[0:n, h // 2, c + P:c + P + n], sm[0:n, h, WIN:WIN + n], ident[0:n, 0:n])
                    last.then_inc(probs_transposed, 1)
                elif s == 21:
                    pe.wait_ge(pT_act, m + 1)
                    pe.wait_ge(pT_dve, m + 1)
                    for h in range(QH):
                        g = h // GRP * HD
                        T.matmul(mx[0:n, 0, h * HD:(h + 1) * HD], pT[:, h, 0, 0:n], vprev[:, g:g + HD], start=True, stop=False)
                        last = T.matmul(mx[0:n, 0, h * HD:(h + 1) * HD], pT[0:n, h, 1, 0:n], pj[0:n, OFF_SV + g:OFF_SV + g + HD], start=False, stop=True)
                    last.then_inc(attn_ready, 1)
                elif s in (23, 30):
                    rows_ = cat if s == 23 else h2
                    pe.wait_ge(cat_ready if s == 23 else h2_ready, m + 1)
                    for k in range(DC):
                        last = T.transpose(mx[:, k // 4, k % 4 * P:k % 4 * P + n], rows_[0:n, k * P:(k + 1) * P], ident[0:n, 0:n])
                    last.then_inc(rows_transposed, 1)
                elif s in (25, 26):
                    half = s - 25
                    if half == 0:
                        pe.wait_ge(t8_act, 2 * m + 1)
                        pe.wait_ge(t8_dve, 2 * m + 1)
                        if isinstance(m, int) and m == 0:
                            pe.wait_ge(w2_in, 32)
                    for k in range(DC):
                        last = T.matmul(mx[0:n, 2 + half, :], t8[:, k, 0:n], wout_s[:, k, half * 512:half * 512 + 512], start=k == 0, stop=k == DC - 1)
                    if half:
                        last.then_inc(mixed_ready, 1)
                elif 32 <= s <= 35:
                    if s == 32:
                        pe.wait_ge(t8_act, 2 * m + 2)
                        pe.wait_ge(t8_dve, 2 * m + 2)
                    for i in range(4):
                        c = 4 * (s - 32) + i
                        for k in range(DC):
                            last = T.matmul(mx[:, s - 32, i * P:i * P + n], wq_s[:, k, c * NK:(c + 1) * NK], t8[:, k, 0:n], start=k == 0, stop=k == DC - 1)
                    last.then_inc(query_ready, 1)
                elif s == 37:
                    pe.wait_ge(qT_ready, 4 * (m + 1))
                    for c in range(QC):
                        last = T.matmul(mx[0:n, c // 4, c % 4 * NK:(c % 4 + 1) * NK], qT[:, c, 0:n], kT[:, c % 2, :], start=True, stop=True)
                    last.then_inc(keys_scored, 1)

            def tile(m, n, nxt):
                pe.wait_ge(x2_ready, m + 1)
                if not (isinstance(m, int) and m == 0):
                    pe.wait_ge(y_ready, m)
                for half in range(2):
                    last = T.matmul(acc[:, half * 512:half * 512 + 512], ident[:, :], xt[:, half * 512:half * 512 + 512], start=True, stop=False)
                last.then_inc(acc_set, 1)
                for h in range(PH):
                    g = PH * m + h
                    for k in range(TOPK):
                        pe.wait_ge(v_in[k % NV], 16 * (TOPK // NV * g + k // NV + 1))
                        pe.wait_ge(diag_ready, TOPK * g + k + 1)
                        end = h == PH - 1 and k == TOPK - 1
                        for half in range(2):
                            last = T.matmul(acc[:, half * 512:half * 512 + 512], diag[0:n, k % NV, :],
                                            ring[0:n, NU + k % NV, half * 512:half * 512 + 512], start=False, stop=end)
                        last.then_inc(v_free, 1)
                        if end:
                            pe.drain().then_inc(acc_done, 1)
                        if nxt:
                            for s in step_at(TOPK * h + k):
                                mix(s, *nxt)

            for s in range(STEPS):
                mix(s, 0, DEC)
            store_state(1)
            tile(0, DEC, (1, P))
            with pe.Fori(0, TILES - 2) as j:
                tile(j + 1, P, (j + 2, P))
            store_state(2)
            tile(TILES - 1, P, None)


_INS = ["x_prompt", "x_sample", "cache_swa_k", "cache_swa_v", "state_mlstm_c", "state_mlstm_n", "state_mlstm_m",
        "norm_mix_w", "w_in", "mlstm_if_bias", "mlstm_norm_w", "swa_sinks", "w_out", "norm_ffn_w", "peer_w_q",
        "peer_sub_keys_1", "peer_sub_keys_2", "peer_u", "peer_v", "norm_final_w"]
_OUTS = [(TILES * P, D), (1, 1, WIN, KVH, HD), (1, 1, WIN, KVH, HD), (1, 1, MH, MD, MD), (1, 1, MH, MD), (1, 1, MH),
         (1, 1, WIN, KVH, HD), (1, 1, WIN, KVH, HD), (1, 1, MH, MD, MD), (1, 1, MH, MD), (1, 1, MH)]


def rotation_table():
    pos = np.zeros(TILES * P, np.float32)
    pos[:DEC] = PAST + np.arange(DEC)
    pos[P:] = np.arange(SEQ)
    inv = np.float32(THETA) ** (-np.arange(ROT, dtype=np.float32) * np.float32(2.0) / np.float32(2 * ROT))
    ang = (pos[:, None] * inv[None, :].astype(np.float32)).astype(np.float32)
    return np.concatenate([np.cos(ang), np.sin(ang)], axis=1).astype(np.float32)


def kernel(**inputs):
    import concourse.bacc as _bacc
    from concourse.bass_utils import run_bass_kernel_spmd as _run

    nc = _bacc.Bacc("TRN2", target_bir_lowering=False, num_devices=1)
    arrays, args = {}, []
    for name in _INS + ["rotation"]:
        a = rotation_table() if name == "rotation" else np.ascontiguousarray(inputs[name])
        arrays[f"in_{name}_dram"] = a
        args.append(nc.dram_tensor(f"in_{name}_dram", a.shape, mybir.dt.from_np(a.dtype), kind="ExternalInput").ap())
    for i, shape in enumerate(_OUTS):
        args.append(nc.dram_tensor(f"out_{i}_dram", shape, F32, kind="ExternalOutput").ap())
    program(nc, *args)
    r = _run(nc, [arrays], core_ids=[0]).results[0]
    got = [r[f"out_{i}_dram"] for i in range(len(_OUTS))]
    y = got[0]
    return (y[P:].reshape(1, SEQ, D), y[:DEC].reshape(1, DEC, D), *got[1:])
```

```python
from contextlib import ExitStack

import concourse.bass as bass
import numpy as np
from concourse import mybir

F32 = mybir.dt.float32
U32 = mybir.dt.uint32
I32 = mybir.dt.int32
ALU = mybir.AluOpType
ACT = mybir.ActivationFunctionType
AX = mybir.AxisListType

P = 128
D = 1024
DC = D // P
SEQ = 1024
DEC = 32
PAST = 512
MH, MD = 4, 128
MW = MH * MD
QH, KVH, HD = 8, 2, 64
GRP = QH // KVH
WIN = 128
CHUNK = 64
ROT = 8
THETA = 500000.0
COLS = 4 * MW + 2 * MH + QH * HD + 2 * KVH * HD
OFF_Q, OFF_K, OFF_V, OFF_O = 0, MW, 2 * MW, 3 * MW
OFF_G = 4 * MW
OFF_SQ = OFF_G + 2 * MH
OFF_SK = OFF_SQ + QH * HD
OFF_SV = OFF_SK + KVH * HD
PH, NK, TOPK = 8, 128, 16
QC = 2 * PH
EPS = 1e-6
BIG = 1e30
LOW = -3.0e38
TILES = 1 + SEQ // P
NU = 4
NV = 4
PC = [(c, min(512, COLS - c)) for c in range(0, COLS, 512)]
BEFORE_OUT = ["gates", "qk_transpose", "qk_copy", "gate_sums", "running_max", "spread_max", "decay_matrix", "decay_weights",
              "mlstm_products", "state_part", "mlstm_out", "new_state", "rotate", "order_heads", "attn_transpose", "attn_copy",
              "attn_scores", "softmax_max", "softmax_exp", "probs_transpose", "probs_copy", "attn_out", "concat",
              "cat_transpose", "cat_copy"]
EARLY = [(s, 0) for s in BEFORE_OUT]
LATE = [("out_proj", i) for i in range(8)]
LATE += [(s, 0) for s in ("residual", "norm_root", "normalise", "h2_transpose", "h2_copy")]
LATE += [("query", i) for i in range(5)] + [("query_copy", 0)] + [("query", i) for i in range(5, 9)] + [("query_copy", 1)]
LATE += [("query", i) for i in range(9, 13)] + [("query_copy", 2)] + [("query", i) for i in range(13, 16)]
LATE += [("query_copy", 3), ("score_keys", 0), ("score_keys", 1), ("keep_scores", 0)]
STEPS = EARLY + LATE
SPREAD = 96
AHEAD = 15
LAG = TOPK + 2
BESIDE = [EARLY[a:b] for a, b in ((0, 2), (2, 4), (4, 6), (6, 9), (9, 11), (11, 15), (15, 17), (17, 20), (20, 22), (22, 24), (24, 25), (25, 25))]


def heads_of(m):
    return PH * DEC // P if isinstance(m, int) and m == 0 else PH


def heads_before(m):
    return 0 if isinstance(m, int) and m == 0 else PH * m - (PH - PH * DEC // P)


def ring_head(m, h):
    return h if isinstance(m, int) and m == 0 else h + PH * DEC // P


def step_at(slot, m):
    if isinstance(m, int) and m == 0:
        rest = STEPS[AHEAD:]
        return [s for i, s in enumerate(rest) if i * TOPK // len(rest) == slot]
    return [s for i, s in enumerate(STEPS) if i * SPREAD // len(STEPS) == slot]


def program(nc, x_prompt, x_sample, cache_k, cache_v, st_c, st_n, st_m, norm_mix_w, w_in, if_bias, mnorm_w, sinks,
            w_out, norm_ffn_w, w_q, keys_1, keys_2, peer_u, peer_v, norm_final_w, rot_tab,
            y, kp, vp, cp, np_, mp, ks, vs, cs, ns, ms):
    xp_d = x_prompt.rearrange("a s d -> (a s) d")
    xs_d = x_sample.rearrange("a s d -> (a s) d")
    u_d = peer_u.rearrange("a e d -> (a e) d")
    v_d = peer_v.rearrange("a e d -> (a e) d")
    proj_d = nc.dram_tensor("proj_scratch", (TILES * P, COLS), F32, kind="Internal").ap()

    with ExitStack() as ctx:
        def sb(name, shape, dt=F32):
            return ctx.enter_context(nc.sbuf_tensor(name, shape, dt))

        def sem(name):
            return ctx.enter_context(nc.semaphore(name))

        weights = sb("weights", [P, DC * 2 * PH * NK + DC * D])
        win_s = [weights[:, DC * c0:DC * (c0 + w)].rearrange("p (k c) -> p k c", k=DC) for c0, w in PC]
        wout_s = weights[:, 0:DC * D].rearrange("p (k c) -> p k c", k=DC)
        wq_s = weights[:, DC * D:].rearrange("p (k c) -> p k c", k=DC)
        ring = sb("ring", [P, NU + NV, D])
        pj = sb("pj", [P, COLS])
        xt = sb("xt", [P, D])
        cat = sb("cat", [P, D])
        h2 = sb("h2", [P, D])
        reg = sb("reg", [P, 3588])
        qkT = reg[:, 0:1024].rearrange("p (h t) -> p h t", h=8)
        dT = reg[:, 1024:1536].rearrange("p (h t) -> p h t", h=MH)
        wT = reg[:, 1536:2048].rearrange("p (h t) -> p h t", h=MH)
        num = reg[:, 2048:2048 + MH * 129].rearrange("p (h e) -> p h e", h=MH)
        hm = reg[:, 2564:3076].rearrange("p (h e) -> p h e", h=MH)
        sq = reg[:, 3076:3588].rearrange("p (h e) -> p h e", h=MH)
        qr = reg[:, 0:512].rearrange("p (j g d) -> p j g d", j=GRP, g=KVH)
        qTs = reg[:, 512:1024].rearrange("p (j t) -> p j t", j=GRP)
        sm = reg[:, 1024:3072].rearrange("p (h s) -> p h s", h=QH)
        t8 = reg[:, 0:1024].rearrange("p (k t) -> p k t", k=DC)
        pT = pj[:, 0:2048].rearrange("p (h b t) -> p h b t", h=QH, b=2)
        qT = pj[:, 0:2048].rearrange("p (c t) -> p c t", c=QC)
        vx = sb("vx", [P, MH, 129])
        ct = sb("ct", [P, MH, 129])
        mb = sb("mb", [P, MH])
        mrow = sb("mrow", [MH, 1])
        ktw = sb("ktw", [P, 2 * P])
        vprev = sb("vprev", [P, P])
        kprev = sb("kprev", [P, P])
        sc = sb("sc", [P, QC, NK])
        rot = sb("rot", [P, 2 * ROT])
        rt = reg[:, 1024:1024 + 4 * (QH + KVH) * ROT].rearrange("p (i h r) -> p i h r", i=4, r=ROT)
        g8 = sb("g8", [P, 8])
        gab = sb("gab", [P, 3, MH])
        lf = sb("lf", [P, 2, MH])
        acol = sb("acol", [P, MH])
        bsum = sb("bsum", [P, 8])
        rows = sb("rows", [MH, 3, P])
        ea = sb("ea", [P, 12])
        ex = sb("ex", [P, 12])
        d4 = sb("d4", [P, 5, MH])
        s8 = sb("s8", [P, 6, QH])
        nr = sb("nr", [P, 4])
        t2 = sb("t2", [P, 2, TOPK])
        i2 = sb("i2", [P, 2, TOPK], U32)
        i2f = sb("i2f", [P, 2, TOPK])
        cand = sb("cand", [P, TOPK, TOPK])
        top = sb("top", [P, 2, TOPK])
        sel = sb("sel", [P, TOPK], U32)
        ij = sb("ij", [P, 2, TOPK], U32)
        oh = sb("oh", [P, 2, TOPK, TOPK])
        r2 = sb("r2", [P, 2, TOPK])
        idx = sb("idx", [P, 4, TOPK], U32)
        ntop = sb("ntop", [P, 2])
        ew = sb("ew", [P, TOPK])
        ez = sb("ez", [P, 2])
        dots = sb("dots", [P, 2, TOPK])
        gl = sb("gl", [P, TOPK])
        coef = sb("coef", [P, 2, TOPK])
        diag = sb("diag", [P, NV, P])
        yo = sb("yo", [P, D])
        yr = sb("yr", [P, 3])
        ident = sb("ident", [P, P])
        triu = sb("triu", [P, P])
        rept = sb("rept", [P, P])
        dmask = sb("dmask", [P, P])
        ones = sb("ones", [P, P])
        wmask = sb("wmask", [P, 2, 2 * P])
        iota_i = sb("iota_i", [P, TOPK], I32)
        iota = sb("iota", [P, TOPK])
        bias8 = sb("bias8", [P, 8])
        sink8 = sb("sink8", [P, QH])
        mnw = sb("mnw", [P, MW])
        ffw = sb("ffw", [P, D])
        fiw = sb("fiw", [P, D])
        kT = sb("kT", [P, 2, NK])
        epsc = sb("epsc", [P, 1])
        x1 = [ring[:, b, :] for b in range(2)]
        h1 = [ring[:, 2 + b, :] for b in range(2)]
        hT1 = [ring[:, 4 + b, :].rearrange("p (k t) -> p k t", k=DC) for b in range(2)]
        nmw = ring[:, 6, :]
        po = [(sc[:, :, :].rearrange("p c k -> p (c k)") if c < 4 else yo)[:, c % 4 * 512:c % 4 * 512 + PC[c][1]] for c in range(6)]

        mx = ctx.enter_context(nc.psum_tensor("mx", [P, 4, 512], F32))
        h2p = ctx.enter_context(nc.psum_tensor("h2p", [P, D], F32))
        acc = ctx.enter_context(nc.psum_tensor("acc", [P, D], F32))
        pbank = [acc[:, c % 2 * 512:c % 2 * 512 + PC[c][1]] for c in range(6)]
        bcol, blast = mx[:, 0, 0:4], mx[:, 0, 4:8]
        gcol, glast = mx[:, 0, 8:12], mx[:, 0, 12:16]
        brow, arow = mx[0:MH, 0, 16:144], mx[0:MH, 0, 144:272]

        const_in, pool_const, const_ready = sem("const_in"), sem("pool_const"), sem("const_ready")
        win_in, x1_in = [sem(f"win_in{c}") for c in range(6)], [sem("x1_in0"), sem("x1_in1")]
        rms1_ready, h1_ready, h1_transposed = sem("rms1_ready"), sem("h1_ready"), sem("h1_transposed")
        hT1_act, hT1_dve, chunk_ready = sem("hT1_act"), sem("hT1_dve"), sem("chunk_ready")
        chunk_act, chunk_dve = sem("chunk_act"), sem("chunk_dve")
        proj_out = [sem(f"proj_out{c}") for c in range(6)]
        wout_in, wq_in, h2p_set = sem("wout_in"), sem("wq_in"), sem("h2p_set")
        keysT_ready = sem("keysT_ready")
        state_in, stateT_ready, state_set = sem("state_in"), sem("stateT_ready"), sem("state_set")
        p_in, x_in = sem("p_in"), sem("x_in")
        gates_ready, softplus_ready, lf_ready = sem("gates_ready"), sem("softplus_ready"), sem("lf_ready")
        qk_transposed, mqT_ready, mkT_ready = sem("qk_transposed"), sem("mqT_ready"), sem("mkT_ready")
        sums_ready, qk_ready, grow_ready = sem("sums_ready"), sem("qk_ready"), sem("grow_ready")
        gb_ready, dT_ready, exparg_ready, ex_ready = sem("gb_ready"), sem("dT_ready"), sem("exparg_ready"), sem("ex_ready")
        wT_ready, num_ready, inter_ready = sem("wT_ready"), sem("num_ready"), sem("inter_ready")
        ssq_ready, dc_ready, state_ready, mrms_ready = sem("ssq_ready"), sem("dc_ready"), sem("state_ready"), sem("mrms_ready")
        rope_ready, qr_ready, swa_transposed = sem("rope_ready"), sem("qr_ready"), sem("swa_transposed")
        sqT_ready, skT_ready, swa_scored = sem("sqT_ready"), sem("skT_ready"), sem("swa_scored")
        smarg_ready, probs_ready, probs_transposed = sem("smarg_ready"), sem("probs_ready"), sem("probs_transposed")
        pT_act, pT_dve, attn_ready, cat_ready = sem("pT_act"), sem("pT_dve"), sem("attn_ready"), sem("cat_ready")
        rows_transposed, t8_act, t8_dve = sem("rows_transposed"), sem("t8_act"), sem("t8_dve")
        mixed_ready, x2_ready, rms2_ready, h2_ready = sem("mixed_ready"), sem("x2_ready"), sem("rms2_ready"), sem("h2_ready")
        query_ready, qT_ready, keys_scored, sc_ready = sem("query_ready"), sem("qT_ready"), sem("keys_scored"), sem("sc_ready")
        topk_done, pool_step, dve_step = sem("topk_done"), sem("pool_step"), sem("dve_step")
        u_in = [sem(f"u_in{i}") for i in range(NU)]
        v_in = [sem(f"v_in{i}") for i in range(NV)]
        u_free, v_free = sem("u_free"), sem("v_free")
        dots_done, gelu_ready, coef_ready, diag_ready = sem("dots_done"), sem("gelu_ready"), sem("coef_ready"), sem("diag_ready")
        acc_set, acc_done, yrms_ready, y_ready, y_out = sem("acc_set"), sem("acc_done"), sem("yrms_ready"), sem("y_ready"), sem("y_out")
        outs_done, st_ready, st_copied, st_out = sem("outs_done"), sem("st_ready"), sem("st_copied"), sem("st_out")

        def copy_probs(eng, half, n):
            copy = eng.copy if half == 0 else eng.tensor_copy
            src = mx[:, 2 * half:2 * half + 2, :].rearrange("p b (h w t) -> p (b h) w t", h=2, w=2)
            dst = pT[:, 4 * half:4 * half + 4, :, :]
            copy(dst[:, :, 0, 0:n], src[:, :, 0, 0:n])
            copy(dst[0:n, :, 1, 0:n], src[0:n, :, 1, 0:n])

        block = ctx.enter_context(nc.Block())

        @block.sync
        def _(sp):
            def load_x1(m, b):
                if not isinstance(m, int) or m >= 2:
                    sp.wait_ge(h1_ready, m - 1)
                if isinstance(m, int) and m == 0:
                    sp.dma_start(x1[b][0:DEC, :], xs_d).then_inc(x1_in[b], 16)
                else:
                    sp.dma_start(x1[b], xp_d[bass.ds((m - 1) * P, P), :]).then_inc(x1_in[b], 16)

            def load_p(m, n):
                if not (isinstance(m, int) and m == 0):
                    sp.wait_ge(keys_scored, m)
                sp.dma_start(pj[0:n, :], proj_d[bass.ds(m * P, n), :]).then_inc(p_in, 16)
                sp.dma_start(rot[0:n, :], rot_tab[bass.ds(m * P, n), :]).then_inc(p_in, 16)

            def load_x(m):
                sp.wait_ge(acc_set, m)
                sp.dma_start(xt[:, :], xp_d[bass.ds((m - 1) * P, P), :]).then_inc(x_in, 16)

            def store_y(m):
                sp.wait_ge(y_ready, m + 1)
                sp.dma_start(y[bass.ds(m * P, P), :], yo[:, :]).then_inc(y_out, 16)

            def store_state(c, n_, m_, count):
                sp.wait_ge(st_copied, count)
                sp.dma_start(c[0, 0].rearrange("h e d -> e h d"), cat[:, 0:MW].rearrange("e (h d) -> e h d", h=MH)).then_inc(st_out, 16)
                sp.dma_start(n_[0, 0], cat[0:MH, 512:640]).then_inc(st_out, 16)
                sp.dma_start(m_[0, 0].rearrange("(h a) -> h a", a=1), mrow[:, :]).then_inc(st_out, 16)

            load_x1(0, 0)
            for dst, src in ((nmw, norm_mix_w[0]), (ffw[:, :], norm_ffn_w[0]), (fiw[:, :], norm_final_w),
                             (mnw[:, :], mnorm_w[0]), (bias8[:, :], if_bias[0]), (sink8[:, :], sinks[0])):
                sp.dma_start(dst, src.partition_broadcast(P)).then_inc(const_in, 16)
            sp.dma_start(h2[:, 0:P], keys_1[0]).then_inc(const_in, 16)
            sp.dma_start(h2[:, P:2 * P], keys_2[0]).then_inc(const_in, 16)

            for c, (c0, w) in enumerate(PC):
                sp.dma_start(win_s[c], w_in[0, :, c0:c0 + w].rearrange("(k p) c -> p k c", p=P)).then_inc(win_in[c], 16)
                if c == 1:
                    load_x1(1, 1)

            def store_proj(m, n, c):
                sp.wait_ge(chunk_dve if c % 2 else chunk_act, 3 * m + c // 2 + 1)
                c0, w = PC[c]
                sp.dma_start(proj_d[bass.ds(m * P, n), c0:c0 + w], po[c][0:n, :]).then_inc(proj_out[c], 16)

            sp.dma_start(cat[:, 0:MW].rearrange("e (h d) -> e h d", h=MH), st_c[0, 0].rearrange("h e d -> e h d")).then_inc(state_in, 16)
            sp.dma_start(cat[0:MH, 512:640], st_n[0, 0]).then_inc(state_in, 16)
            sp.dma_start(cat[:, 640:768], cache_k[0, 0].rearrange("s g d -> s (g d)")).then_inc(state_in, 16)
            sp.dma_start(vprev[:, :], cache_v[0, 0].rearrange("s g d -> s (g d)")).then_inc(state_in, 16)
            sp.dma_start(mb[:, :], st_m[0, 0].partition_broadcast(P)).then_inc(state_in, 16)
            sp.dma_start(mrow[:, :], st_m[0, 0].rearrange("(h a) -> h a", a=1)).then_inc(state_in, 16)

            sp.wait_ge(pool_const, 1)
            sp.dma_start(xt[0:DEC, :], xs_d).then_inc(x_in, 16)
            for old, new in ((cache_k, ks), (cache_v, vs)):
                sp.dma_start(new[0, 0, 0:WIN - DEC], old[0, 0, DEC:WIN]).then_inc(outs_done, 16)

            load_x1(2, 0)
            for c in range(6):
                store_proj(0, DEC, c)
            for c in range(6):
                sp.wait_ge(proj_out[c], 16)
            load_p(0, DEC)
            for m in (1, 2):
                load_x1(m + 2, m % 2)
                for c in range(6):
                    store_proj(m, P, c)
            with sp.Fori(0, TILES // 2 - 2) as j:
                for i in (0, 1):
                    load_x1(2 * j + i + 5, (i + 1) % 2)
                    for c in range(6):
                        store_proj(2 * j + i + 3, P, c)
            for c in range(6):
                store_proj(TILES - 2, P, c)
            for c in range(6):
                sp.wait_ge(chunk_ready, 6 * (TILES - 1) + c + 1)
                if c == 1:
                    sp.dma_start(wout_s, w_out[0].rearrange("(k p) c -> p k c", p=P)).then_inc(wout_in, 16)
                elif c > 1:
                    k = 2 * (c - 2)
                    sp.dma_start(wq_s[:, k:k + 2, :], w_q[0, k * P:(k + 2) * P, :].rearrange("(k p) c -> p k c", p=P)).then_inc(wq_in, 16)
                store_proj(TILES - 1, P, c)
            for c in range(6):
                sp.wait_ge(proj_out[c], 16 * TILES)
            sp.wait_ge(rope_ready, 1)
            sp.dma_start(ks[0, 0, WIN - DEC:WIN].rearrange("s g d -> s (g d)"), pj[0:DEC, OFF_SK:OFF_SV]).then_inc(outs_done, 16)
            sp.dma_start(vs[0, 0, WIN - DEC:WIN].rearrange("s g d -> s (g d)"), pj[0:DEC, OFF_SV:COLS]).then_inc(outs_done, 16)
            store_state(cs, ns, ms, 1)
            sp.wait_ge(outs_done, 16 * 4)
            load_p(1, P)
            load_x(1)
            with sp.Fori(0, TILES - 2) as j:
                load_p(j + 2, P)
                load_x(j + 2)
                store_y(j)
            store_state(cp, np_, mp, 2)
            sp.dma_start(kp[0, 0].rearrange("s g d -> s (g d)"), kprev[:, :]).then_inc(outs_done, 16)
            sp.dma_start(vp[0, 0].rearrange("s g d -> s (g d)"), vprev[:, :]).then_inc(outs_done, 16)
            store_y(TILES - 2)
            store_y(TILES - 1)
            sp.wait_ge(st_out, 16 * 6)
            sp.wait_ge(outs_done, 16 * 6)
            sp.wait_ge(y_out, 16 * TILES)

        @block.gpsimd
        def _(pool):
            for t, v in ((ident, 0.0), (triu, 1.0), (rept, 0.0), (dmask, 0.0), (ones, 1.0), (wmask, 0.0), (xt, 0.0), (ea, 0.0)):
                pool.memset(t[:], v)
            pool.iota(iota_i[:, :], [[1, TOPK]], base=0, channel_multiplier=0)
            pool.drain()
            pool.affine_select(out=ident[:, :], in_=ident[:, :], compare_op=ALU.not_equal, fill=1.0, base=0,
                               pattern=[[-1, P]], channel_multiplier=1)
            for t, fill in ((triu, 0.0), (dmask, BIG)):
                pool.affine_select(out=t[:, :], in_=t[:, :], compare_op=ALU.is_ge, fill=fill, base=0,
                                   pattern=[[1, P]], channel_multiplier=-1)
            pool.drain()
            pool.memset(wmask[0:CHUNK, :, WIN + CHUNK:], -BIG)
            pool.drain()
            pool.memset(wmask[CHUNK:P, 1, 0:CHUNK], -BIG)
            pool.drain()
            pool.memset(wmask[:, 0, 0:WIN], -BIG)
            pool.drain().then_inc(pool_const, 1)
            pool.sem_inc(u_free, NU)
            pool.sem_inc(v_free, NV)

            def gather_u(g, h, k):
                if k == 0:
                    pool.wait_ge(topk_done, g + 1)
                pool.wait_ge(u_free, TOPK * g + k + 1)
                pool.sem_inc(pool_step, 1)
                pool.indirect_dma_start(ring[:, k % NU, :], None, u_d,
                                        bass.IndirectOffsetOnAxis(ap=idx[:, h % 4, k:k + 1], axis=0)).then_inc(u_in[k % NU], 16)

            def gather_v(g, h, k):
                pool.wait_ge(v_free, TOPK * g + k + 1)
                pool.sem_inc(pool_step, 1)
                pool.indirect_dma_start(ring[:, NU + k % NV, :], None, v_d,
                                        bass.IndirectOffsetOnAxis(ap=idx[:, h % 4, k:k + 1], axis=0)).then_inc(v_in[k % NV], 16)

            def tile(m, last):
                heads = heads_of(m)
                for h in range(heads):
                    g = heads_before(m) + h
                    for k in range(TOPK):
                        if h < heads - 1 or not last:
                            gather_u(g + 1, ring_head(m, h + 1), k)
                        gather_v(g, ring_head(m, h), k)

            for k in range(TOPK):
                gather_u(0, 0, k)
            tile(0, False)
            with pool.Fori(0, TILES - 2) as j:
                tile(j + 1, False)
            tile(TILES - 1, True)

        @block.scalar
        def _(act):
            S = nc.scalar

            def rms1(m, b, n, nth):
                act.wait_ge(x1_in[b], 16 * nth)
                if not (isinstance(m, int) and m == 0):
                    act.wait_ge(h1_ready, m)
                if not (isinstance(m, int) and m < 2):
                    act.wait_ge(chunk_ready, 6 * (m - 1))
                S.activation(hT1[b][0:n, :, :].rearrange("p k t -> p (k t)"), x1[b][0:n, :], ACT.Square, accum_out=nr[0:n, 0:1])
                act.drain()
                S.activation(nr[0:n, 1:2], nr[0:n, 0:1], ACT.Sqrt, scale=1.0 / D, bias=epsc[0:n, 0:1])
                act.drain().then_inc(rms1_ready, 1)

            def hT1_copy(m, b, n):
                act.wait_ge(h1_transposed, m + 1)
                S.copy(hT1[b][:, 0:4, 0:n], h2p[:, 0:512].rearrange("p (k t) -> p k t", k=4)[:, :, 0:n])
                act.drain().then_inc(hT1_act, 1)

            def chunk_copy(m, n, c):
                act.wait_ge(chunk_ready, 6 * m + c + 1)
                if not (isinstance(m, int) and m == 0):
                    act.wait_ge(proj_out[c], 16 * m)
                S.copy(po[c][0:n, :], pbank[c][0:n, :])
                act.drain().then_inc(chunk_act, 1)

            def proj_tile(m, b, n, nth, beside=None, last=False):
                if not last:
                    rms1(m + 1, 1 - b, P, nth)
                for c in range(6):
                    if c == 3 and not last:
                        hT1_copy(m + 1, 1 - b, P)
                    if c % 2 == 0:
                        chunk_copy(m, n, c)
                    for s in beside[c] if beside else ():
                        mix(s, 0, DEC)

            def copy_state_out(count):
                act.wait_ge(st_ready, count)
                S.copy(cat[:, 0:MW], mx[:, 0, :])
                S.copy(cat[0:MH, 512:640], mx[0:MH, 1, 0:P])
                act.drain().then_inc(st_copied, 1)

            def mix(step, m, n):
                s, i = step
                if s == "qk_transpose":
                    act.wait_ge(gates_ready, m + 1)
                    S.activation(gab[0:n, 1, :], gab[0:n, 0, :], ACT.Exp, scale=-1.0)
                    act.drain()
                    S.activation(gab[0:n, 2, :], gab[0:n, 1, :], ACT.Ln, bias=ones[0:n, 0:1])
                    act.drain().then_inc(softplus_ready, 1)
                elif s == "qk_copy":
                    act.wait_ge(qk_transposed, m + 1)
                    S.copy(qkT[:, 0:4, 0:n], mx[:, 2, :].rearrange("p (h t) -> p h t", h=4)[:, :, 0:n])
                    act.drain().then_inc(mqT_ready, 1)
                elif s == "decay_matrix":
                    act.wait_ge(gb_ready, m + 1)
                    for h in range(MH):
                        S.activation(dT[0:n, h, 0:n], mx[0:n, 1, h * P:h * P + n], ACT.Exp, scale=-1.0, bias=acol[0:n, h:h + 1])
                    act.drain().then_inc(dT_ready, 1)
                elif s == "decay_weights":
                    act.wait_ge(exparg_ready, m + 1)
                    S.activation(ex[:, :], ea[:, :], ACT.Exp)
                    act.drain().then_inc(ex_ready, 1)
                elif s == "state_part":
                    act.wait_ge(num_ready, m + 1)
                    for h in range(MH):
                        S.activation(num[0:n, h, :], mx[0:n, 2 + h // 2, h % 2 * 129:h % 2 * 129 + 129], ACT.Copy, scale=ex[0:n, h:h + 1])
                    act.drain().then_inc(inter_ready, 1)
                elif s == "new_state":
                    act.wait_ge(ssq_ready, m + 1)
                    S.activation(d4[0:n, 4, :], d4[0:n, 3, :], ACT.Sqrt, scale=1.0 / MD, bias=epsc[0:n, 0:1])
                    S.activation(pj[0:n, OFF_O:OFF_O + MW], pj[0:n, OFF_O:OFF_O + MW], ACT.Sigmoid)
                    act.drain().then_inc(mrms_ready, 1)
                elif s == "order_heads":
                    act.wait_ge(rope_ready, m + 1)
                    S.copy(qr[0:n], pj[0:n, OFF_SQ:OFF_SK].rearrange("p (g j d) -> p j g d", g=KVH, j=GRP))
                    act.drain().then_inc(qr_ready, 1)
                elif s == "attn_copy":
                    act.wait_ge(swa_transposed, m + 1)
                    S.copy(qTs[:, :, 0:n], mx[:, 0, :].rearrange("p (j t) -> p j t", j=GRP)[:, :, 0:n])
                    act.drain().then_inc(sqT_ready, 1)
                elif s == "softmax_exp":
                    act.wait_ge(smarg_ready, m + 1)
                    keys = WIN + n
                    for h in range(QH):
                        S.activation(sm[0:n, h, 0:keys], sm[0:n, h, 0:keys], ACT.Exp, bias=s8[0:n, 1, h:h + 1], accum_out=s8[0:n, 3, h:h + 1])
                    S.activation(s8[0:n, 4, :], s8[0:n, 2, :], ACT.Exp)
                    act.drain().then_inc(probs_ready, 1)
                elif s == "probs_copy":
                    act.wait_ge(probs_transposed, m + 1)
                    copy_probs(S, 0, n)
                    act.drain().then_inc(pT_act, 1)
                elif s in ("cat_copy", "h2_copy"):
                    second = int(s == "h2_copy")
                    act.wait_ge(rows_transposed, 2 * m + 1 + second)
                    S.copy(t8[:, 0:4, 0:n], mx[:, 0, :].rearrange("p (k t) -> p k t", k=4)[:, :, 0:n])
                    act.drain().then_inc(t8_act, 1)
                elif s == "norm_root":
                    act.wait_ge(x2_ready, m + 1)
                    S.activation(cat[0:n, :], xt[0:n, :], ACT.Square, accum_out=nr[0:n, 0:1])
                    act.drain()
                    S.activation(nr[0:n, 1:2], nr[0:n, 0:1], ACT.Sqrt, scale=1.0 / D, bias=epsc[0:n, 0:1])
                    act.drain().then_inc(rms2_ready, 1)
                elif s == "query_copy":
                    g = i
                    act.wait_ge(query_ready, 4 * m + g + 1)
                    S.copy(qT[:, 4 * g:4 * g + 4, 0:n], mx[:, g, :].rearrange("p (c t) -> p c t", c=4)[:, :, 0:n])
                    act.drain().then_inc(qT_ready, 1)
                elif s == "keep_scores":
                    act.wait_ge(keys_scored, m + 1)
                    if isinstance(m, int) and m == 0:
                        S.copy(sc[:, 0:4, :].rearrange("p c k -> p (c k)"), mx[:, 0, :])
                    else:
                        act.wait_ge(topk_done, heads_before(m))
                        S.copy(sc[:, :, :].rearrange("p c k -> p (c k)"), mx[:, :, :].rearrange("p b c -> p (b c)"))
                    act.drain().then_inc(sc_ready, 1)

            def tile(m, n, nxt):
                one = ident
                if isinstance(m, int) and m == 0:
                    one = rept
                    for s in STEPS[:AHEAD]:
                        mix(s, *nxt)
                for h in range(heads_of(m)):
                    g = heads_before(m) + h
                    act.wait_ge(dots_done, g + 1)
                    act.wait_ge(topk_done, g + 1)
                    S.activation(ew[:, :], top[:, h % 2, :], ACT.Exp, bias=ntop[:, h % 2:h % 2 + 1], accum_out=ez[:, 0:1])
                    S.activation(gl[:, :], dots[:, h % 2, :], ACT.Gelu)
                    act.drain().then_inc(gelu_ready, 1)
                    for k in range(TOPK):
                        if k == 0:
                            act.wait_ge(coef_ready, g + 1)
                        act.wait_ge(v_free, TOPK * g + k + 1)
                        S.activation(diag[:, k % NV, :], one[:, :], ACT.Copy, scale=coef[:, h % 2, k:k + 1])
                        act.drain().then_inc(diag_ready, 1)
                        if nxt:
                            for s in step_at(TOPK * h + k, m):
                                mix(s, *nxt)
                act.wait_ge(acc_done, m + 1)
                if not (isinstance(m, int) and m == 0):
                    act.wait_ge(y_out, 16 * m)
                S.activation(yo[:, :], acc[:, :], ACT.Square, accum_out=yr[:, 0:1])
                act.drain()
                S.activation(yr[:, 1:2], yr[:, 0:1], ACT.Sqrt, scale=1.0 / D, bias=epsc[:, 0:1])
                act.drain().then_inc(yrms_ready, 1)

            act.wait_ge(const_ready, 1)
            rms1(0, 0, DEC, 1)
            hT1_copy(0, 0, DEC)
            proj_tile(0, 0, DEC, 1)
            proj_tile(1, 1, P, 2, BESIDE[:6])
            proj_tile(2, 0, P, 2, BESIDE[6:])
            with act.Fori(0, TILES // 2 - 2) as j:
                proj_tile(2 * j + 3, 1, P, j + 3)
                proj_tile(2 * j + 4, 0, P, j + 3)
            proj_tile(TILES - 2, 1, P, TILES // 2 + 1)
            proj_tile(TILES - 1, 0, P, 0, last=True)
            for s in LATE:
                mix(s, 0, DEC)
            copy_state_out(1)
            tile(0, DEC, (1, P))
            with act.Fori(0, TILES - 2) as j:
                tile(j + 1, P, (j + 2, P))
            copy_state_out(2)
            tile(TILES - 1, P, None)

        @block.vector
        def _(dve):
            V = nc.vector

            def bc(ap, *shape):
                return ap.broadcast_to(list(shape))

            dve.wait_ge(pool_const, 1)
            dve.wait_ge(const_in, 16 * 8)
            V.tensor_copy(iota[:, :], iota_i[:, :])
            V.memset(vx[:, :, 128:129], 1.0)
            V.memset(epsc[:, :], EPS)
            for q in range(P // DEC):
                r = slice(q * DEC, (q + 1) * DEC)
                V.tensor_copy(rept[r, 0:DEC], ident[r, r])
            dve.drain().then_inc(const_ready, 1)

            def norm1(m, b, n):
                dve.wait_ge(rms1_ready, m + 1)
                V.reciprocal(nr[0:n, 2:3], nr[0:n, 1:2])
                dve.drain()
                V.scalar_tensor_tensor(h1[b][0:n, :], x1[b][0:n, :], nr[0:n, 2:3], nmw[0:n, :], ALU.mult, ALU.mult)
                dve.drain().then_inc(h1_ready, 1)

            def hT1_copy(m, b, n):
                dve.wait_ge(h1_transposed, m + 1)
                V.tensor_copy(hT1[b][:, 4:8, 0:n], h2p[:, 512:].rearrange("p (k t) -> p k t", k=4)[:, :, 0:n])
                dve.drain().then_inc(hT1_dve, 1)

            def chunk_copy(m, n, c):
                dve.wait_ge(chunk_ready, 6 * m + c + 1)
                if not (isinstance(m, int) and m == 0):
                    dve.wait_ge(proj_out[c], 16 * m)
                V.tensor_copy(po[c][0:n, :], pbank[c][0:n, :])
                dve.drain().then_inc(chunk_dve, 1)

            def proj_tile(m, b, n, beside=None, last=False):
                if not last:
                    norm1(m + 1, 1 - b, P)
                for c in range(6):
                    if c == 3 and not last:
                        hT1_copy(m + 1, 1 - b, P)
                    if c % 2:
                        chunk_copy(m, n, c)
                    for s in beside[c] if beside else ():
                        mix(s, 0, DEC)

            def set_state():
                dve.wait_ge(keysT_ready, 1)
                V.tensor_copy(kT[:, :, :].rearrange("p a k -> p (a k)"), mx[:, 3, 0:2 * NK])
                dve.wait_ge(stateT_ready, 1)
                V.tensor_copy(ct[:, :, 0:MD], mx[:, 0, :].rearrange("p (h e) -> p h e", h=MH))
                V.tensor_copy(ct[:, :, MD:MD + 1], mx[:, 1, 0:MH].rearrange("p (h a) -> p h a", a=1))
                V.tensor_copy(ktw[:, 0:P], mx[:, 2, 0:P])
                dve.drain().then_inc(state_set, 1)

            def mix(step, m, n):
                s, i = step
                if s == "gates":
                    dve.wait_ge(p_in, 32 * (m + 1))
                    V.tensor_tensor(g8[0:n, :], pj[0:n, OFF_G:OFF_SQ], bias8[0:n, :], ALU.add)
                    V.tensor_scalar(pj[0:n, OFF_K:OFF_V], pj[0:n, OFF_K:OFF_V], MD ** -0.5, None, ALU.mult)
                    V.tensor_copy(vx[0:n, :, 0:MD], pj[0:n, OFF_V:OFF_O].rearrange("p (h e) -> p h e", h=MH))
                    dve.drain()
                    V.scalar_tensor_tensor(gab[0:n, 0, :], g8[0:n, 4:8], -1.0, g8[0:n, 4:8], ALU.mult, ALU.max)
                    dve.drain().then_inc(gates_ready, 1)
                elif s == "qk_copy":
                    dve.wait_ge(softplus_ready, m + 1)
                    V.scalar_tensor_tensor(lf[0:n, 0, :], g8[0:n, 4:8], 0.0, gab[0:n, 2, :], ALU.min, ALU.subtract)
                    dve.drain()
                    V.tensor_scalar(lf[0:n, 1, :], lf[0:n, 0, :], -1.0, None, ALU.mult)
                    dve.drain().then_inc(lf_ready, 1)
                    dve.wait_ge(qk_transposed, m + 1)
                    V.tensor_copy(qkT[:, 4:8, 0:n], mx[:, 3, :].rearrange("p (h t) -> p h t", h=4)[:, :, 0:n])
                    dve.drain().then_inc(mkT_ready, 1)
                elif s == "running_max":
                    dve.wait_ge(sums_ready, m + 1)
                    V.tensor_copy(bsum[0:n, 0:4], bcol[0:n, :])
                    V.tensor_copy(bsum[:, 4:8], blast)
                    V.tensor_copy(rows[:, 0, 0:n], brow[:, 0:n])
                    V.tensor_copy(rows[:, 1, 0:n], arow[:, 0:n])
                    dve.drain()
                    V.tensor_tensor(acol[0:n, :], g8[0:n, 0:4], bsum[0:n, 0:4], ALU.subtract)
                    V.tensor_tensor_scan(rows[:, 2, 0:n], rows[:, 1, 0:n], rows[:, 1, 0:n], mrow[:, :], ALU.max, ALU.max)
                    dve.drain()
                    V.tensor_tensor(mrow[:, :], rows[:, 0, n - 1:n], rows[:, 2, n - 1:n], ALU.add)
                    dve.drain().then_inc(grow_ready, 1)
                elif s == "decay_matrix":
                    dve.wait_ge(gb_ready, m + 1)
                    V.tensor_tensor(ea[0:n, 0:4], mb[0:n, :], gcol[0:n, :], ALU.subtract)
                    V.scalar_tensor_tensor(ea[0:n, 4:8], gcol[0:n, :], -1.0, bsum[0:n, 0:4], ALU.mult, ALU.subtract)
                    V.tensor_tensor(ea[:, 8:12], mb[:, :], glast, ALU.subtract)
                    dve.drain()
                    V.tensor_tensor(mb[:, :], bsum[:, 4:8], glast, ALU.add)
                    dve.drain().then_inc(exparg_ready, 1)
                elif s == "decay_weights":
                    dve.wait_ge(dT_ready, m + 1)
                    dve.wait_ge(qk_ready, m + 1)
                    V.tensor_tensor(wT[0:n, :, 0:n], mx[0:n, 2, :].rearrange("p (h t) -> p h t", h=MH)[:, :, 0:n], dT[0:n, :, 0:n], ALU.mult)
                    pk = pj[0:n, OFF_K:OFF_V].rearrange("p (h d) -> p h d", h=MH)
                    V.tensor_tensor(pk, pk, bc(dT[0:n, :, n - 1:n], n, MH, MD), ALU.mult)
                    dve.drain().then_inc(wT_ready, 1)
                elif s == "mlstm_out":
                    dve.wait_ge(inter_ready, m + 1)
                    dve.wait_ge(ex_ready, m + 1)
                    pair = num[0:n, :, :].rearrange("p (b h) e -> p b (h e)", b=2)
                    V.tensor_tensor(pair, pair, mx[0:n, 0:2, 0:258], ALU.add)
                    dve.drain()
                    den = num[0:n, :, MD:MD + 1].rearrange("p h a -> p (h a)")
                    V.scalar_tensor_tensor(d4[0:n, 0, :], den, -1.0, den, ALU.mult, ALU.max)
                    dve.drain()
                    V.tensor_tensor(d4[0:n, 1, :], d4[0:n, 0, :], ex[0:n, 4:8], ALU.max)
                    dve.drain()
                    V.reciprocal(d4[0:n, 2, :], d4[0:n, 1, :])
                    dve.drain()
                    V.tensor_tensor(hm[0:n, :, :], num[0:n, :, 0:MD], bc(d4[0:n, 2, :].unsqueeze(2), n, MH, MD), ALU.mult)
                    dve.drain()
                    V.tensor_tensor(sq[0:n, :, :], hm[0:n, :, :], hm[0:n, :, :], ALU.mult)
                    dve.drain()
                    V.tensor_reduce(d4[0:n, 3, :], sq[0:n, :, :], AX.X, ALU.add)
                    dve.drain().then_inc(ssq_ready, 1)
                elif s == "new_state":
                    dve.wait_ge(dc_ready, m + 1)
                    for h in range(MH):
                        V.scalar_tensor_tensor(ct[:, h, :], ct[:, h, :], ex[:, 8 + h:9 + h], mx[:, 2 + h // 2, h % 2 * 129:h % 2 * 129 + 129], ALU.mult, ALU.add)
                    dve.drain().then_inc(state_ready, 1)
                elif s == "rotate":
                    dve.wait_ge(mrms_ready, m + 1)
                    V.reciprocal(d4[0:n, 0, :], d4[0:n, 4, :])
                    qk = pj[0:n, OFF_SQ:OFF_SV].rearrange("p (h d) -> p h d", d=HD)
                    xa, xb = qk[:, :, 0:ROT], qk[:, :, ROT:2 * ROT]
                    cos = bc(rot[0:n, 0:ROT].unsqueeze(1), n, QH + KVH, ROT)
                    sin = bc(rot[0:n, ROT:2 * ROT].unsqueeze(1), n, QH + KVH, ROT)
                    for j, (a, b) in enumerate(((xa, cos), (xb, sin), (xb, cos), (xa, sin))):
                        V.tensor_tensor(rt[0:n, j], a, b, ALU.mult)
                    dve.drain()
                    V.tensor_tensor(xa, rt[0:n, 0], rt[0:n, 1], ALU.subtract)
                    V.tensor_tensor(xb, rt[0:n, 2], rt[0:n, 3], ALU.add)
                    V.tensor_tensor(sq[0:n, :, :], hm[0:n, :, :], bc(d4[0:n, 0, :].unsqueeze(2), n, MH, MD), ALU.mult)
                    dve.drain().then_inc(rope_ready, 1)
                    V.tensor_tensor(hm[0:n, :, :].rearrange("p h e -> p (h e)"), sq[0:n, :, :].rearrange("p h e -> p (h e)"), mnw[0:n, :], ALU.mult)
                    dve.drain()
                    V.tensor_tensor(cat[0:n, 0:MW], hm[0:n, :, :].rearrange("p h e -> p (h e)"), pj[0:n, OFF_O:OFF_O + MW], ALU.mult)
                elif s == "attn_copy":
                    dve.wait_ge(swa_transposed, m + 1)
                    V.tensor_copy(ktw[:, WIN:WIN + n], mx[:, 1, 0:n])
                    dve.drain().then_inc(skT_ready, 1)
                elif s == "softmax_max":
                    dve.wait_ge(swa_scored, m + 1)
                    keys = WIN + n
                    scores = mx[0:n, :, :].rearrange("p b (h s) -> p (b h) s", h=2)[:, :, 0:keys]
                    if n == P:
                        V.scalar_tensor_tensor(sm[0:n, :, 0:keys], scores, HD ** -0.5, bc(wmask[0:n, 0:1, 0:keys], n, QH, keys), ALU.mult, ALU.add)
                    else:
                        V.tensor_scalar(sm[0:n, :, 0:keys], scores, HD ** -0.5, None, ALU.mult)
                    dve.drain()
                    V.tensor_reduce(s8[0:n, 0, :], sm[0:n, :, 0:keys], AX.X, ALU.max)
                    dve.drain()
                    V.tensor_tensor(s8[0:n, 5, :], s8[0:n, 0, :], sink8[0:n, :], ALU.max)
                    dve.drain()
                    V.tensor_scalar(s8[0:n, 1, :], s8[0:n, 5, :], -1.0, None, ALU.mult)
                    V.tensor_tensor(s8[0:n, 2, :], sink8[0:n, :], s8[0:n, 5, :], ALU.subtract)
                    dve.drain().then_inc(smarg_ready, 1)
                elif s == "probs_transpose":
                    dve.wait_ge(probs_ready, m + 1)
                    V.tensor_tensor(s8[0:n, 0, :], s8[0:n, 3, :], s8[0:n, 4, :], ALU.add)
                    dve.drain()
                    V.reciprocal(s8[0:n, 5, :], s8[0:n, 0, :])
                elif s == "probs_copy":
                    dve.wait_ge(probs_transposed, m + 1)
                    copy_probs(V, 1, n)
                    dve.drain().then_inc(pT_dve, 1)
                elif s == "concat":
                    dve.wait_ge(attn_ready, m + 1)
                    V.tensor_tensor(cat[0:n, MW:D].rearrange("p (h d) -> p h d", h=QH), mx[0:n, 0, :].rearrange("p (h d) -> p h d", h=QH),
                                    bc(s8[0:n, 5, :].unsqueeze(2), n, QH, HD), ALU.mult)
                    if n == P:
                        V.tensor_copy(ktw[:, 0:WIN], ktw[:, WIN:2 * WIN])
                        V.tensor_copy(vprev[:, :], pj[:, OFF_SV:COLS])
                        V.tensor_copy(kprev[:, :], pj[:, OFF_SK:OFF_SV])
                        V.tensor_copy(wmask[:, 0, :], wmask[:, 1, :])
                    dve.drain().then_inc(cat_ready, 1)
                elif s in ("cat_copy", "h2_copy"):
                    second = int(s == "h2_copy")
                    dve.wait_ge(rows_transposed, 2 * m + 1 + second)
                    V.tensor_copy(t8[:, 4:8, 0:n], mx[:, 1, :].rearrange("p (k t) -> p k t", k=4)[:, :, 0:n])
                    dve.drain().then_inc(t8_dve, 1)
                elif s == "residual":
                    dve.wait_ge(mixed_ready, m + 1)
                    dve.wait_ge(x_in, 16 * (m + 1))
                    V.tensor_tensor(xt[0:n, :], xt[0:n, :], mx[0:n, 2:4, :].rearrange("p b c -> p (b c)"), ALU.add)
                    dve.drain().then_inc(x2_ready, 1)
                elif s == "normalise":
                    dve.wait_ge(rms2_ready, m + 1)
                    V.reciprocal(nr[0:n, 2:3], nr[0:n, 1:2])
                    dve.drain()
                    V.scalar_tensor_tensor(h2[0:n, :], xt[0:n, :], nr[0:n, 2:3], ffw[0:n, :], ALU.mult, ALU.mult)
                    dve.drain().then_inc(h2_ready, 1)

            def topk(h, turn, part, m=None):
                s1, s2 = sc[:, 2 * h, :], sc[:, 2 * h + 1, :]
                cd = cand[:, :, :].rearrange("p a b -> p (a b)")
                tp = top[:, h % 2, :]
                dve.drain()
                if part == 0:
                    if m is not None:
                        dve.wait_ge(sc_ready, m + 1)
                        dve.sem_inc(dve_step, 1)
                    V.max(t2[:, 0, 0:8], s1)
                    V.max(t2[:, 1, 0:8], s2)
                    dve.drain()
                    V.max_index(i2[:, 0, 0:8], t2[:, 0, 0:8], s1)
                    V.max_index(i2[:, 1, 0:8], t2[:, 1, 0:8], s2)
                elif part == 1:
                    V.match_replace(s1, t2[:, 0, 0:8], s1, LOW)
                    V.match_replace(s2, t2[:, 1, 0:8], s2, LOW)
                    dve.drain()
                    V.max(t2[:, 0, 8:16], s1)
                    V.max(t2[:, 1, 8:16], s2)
                elif part == 2:
                    V.max_index(i2[:, 0, 8:16], t2[:, 0, 8:16], s1)
                    V.max_index(i2[:, 1, 8:16], t2[:, 1, 8:16], s2)
                    V.tensor_tensor(cand[:, :, :], bc(t2[:, 0, :].unsqueeze(2), P, TOPK, TOPK), bc(t2[:, 1, :].unsqueeze(1), P, TOPK, TOPK), ALU.add)
                    dve.drain()
                    V.tensor_copy(i2f[:, :, :], i2[:, :, :])
                elif part == 3:
                    V.max(tp[:, 0:8], cd)
                elif part == 4:
                    V.max_index(sel[:, 0:8], tp[:, 0:8], cd)
                    V.tensor_scalar(ntop[:, h % 2:h % 2 + 1], tp[:, 0:1], -1.0, None, ALU.mult)
                elif part == 5:
                    V.match_replace(cd, tp[:, 0:8], cd, LOW)
                elif part == 6:
                    V.max(tp[:, 8:16], cd)
                elif part == 7:
                    V.max_index(sel[:, 8:16], tp[:, 8:16], cd)
                elif part == 8:
                    V.tensor_scalar(ij[:, 0, :], sel[:, :], 4, None, ALU.logical_shift_right)
                    V.tensor_scalar(ij[:, 1, :], sel[:, :], 15, None, ALU.bitwise_and)
                    dve.drain()
                    for a in range(2):
                        V.tensor_tensor(oh[:, a], bc(ij[:, a, :].unsqueeze(2), P, TOPK, TOPK), bc(iota[:, :].unsqueeze(1), P, TOPK, TOPK), ALU.is_equal)
                elif part == 9:
                    for a in range(2):
                        V.tensor_tensor(oh[:, a], oh[:, a], bc(i2f[:, a, :].unsqueeze(1), P, TOPK, TOPK), ALU.mult)
                    dve.drain()
                    V.tensor_reduce(r2[:, :, :], oh[:, :, :, :], AX.X, ALU.add)
                elif part == 10:
                    V.scalar_tensor_tensor(idx[:, turn % 4, :], r2[:, 0, :], float(NK), r2[:, 1, :], ALU.mult, ALU.add)
                    dve.drain().then_inc(topk_done, 1)

            def weigh(g, h):
                dve.wait_ge(gelu_ready, g + 1)
                V.reciprocal(ez[:, 1:2], ez[:, 0:1])
                dve.drain()
                V.scalar_tensor_tensor(coef[:, h % 2, :], gl[:, :], ez[:, 1:2], ew[:, :], ALU.mult, ALU.mult)
                dve.drain().then_inc(coef_ready, 1)

            def finish(m):
                dve.wait_ge(yrms_ready, m + 1)
                V.reciprocal(yr[:, 2:3], yr[:, 1:2])
                dve.drain()
                V.scalar_tensor_tensor(yo[:, :], acc[:, :], yr[:, 2:3], fiw[:, :], ALU.mult, ALU.mult)
                dve.drain().then_inc(y_ready, 1)

            def tile(m, n, nxt):
                first = isinstance(m, int) and m == 0
                if first:
                    dve.wait_ge(h2p_set, 1)
                else:
                    dve.drain()
                    V.tensor_copy(h2p[:, :], h2[:, :])
                    dve.drain()
                heads = heads_of(m)
                for h in range(heads):
                    g = heads_before(m) + h
                    for k in range(TOPK):
                        dve.wait_ge(u_in[k % NU], 16 * (TOPK // NU * g + k // NU + 1))
                        V.scalar_tensor_tensor(ring[:, k % NU, :], ring[:, k % NU, :], 1.0, h2p[:, :], ALU.mult, ALU.mult,
                                               accum_out=dots[:, h % 2, k:k + 1]).then_inc(u_free, 1)
                        if k == TOPK - 1:
                            dve.drain().then_inc(dots_done, 1)
                        if k == 1 and not (first and h == 0):
                            weigh(g - 1, (h - 1) % 2)
                        if k == 1 and h == 1 and not first:
                            finish(m - 1)
                        if k <= 10 and h < heads - 1:
                            topk(h + 1, ring_head(m, h + 1), k)
                        elif k <= 10 and nxt and not first:
                            topk(0, ring_head(1, 0), k, m + 1)
                        if first and h == 0:
                            for s in STEPS[k:min(k + 1, AHEAD)]:
                                mix(s, *nxt)
                        slot = TOPK * h + k - LAG
                        if nxt and slot >= 0:
                            for s in step_at(slot, m):
                                mix(s, *nxt)
                if first:
                    for slot in range(TOPK * heads - LAG, TOPK * heads):
                        for s in step_at(slot, m):
                            mix(s, *nxt)
                    for part in range(11):
                        topk(0, ring_head(1, 0), part, 1)

            norm1(0, 0, DEC)
            hT1_copy(0, 0, DEC)
            proj_tile(0, 0, DEC)
            set_state()
            proj_tile(1, 1, P, BESIDE[:6])
            proj_tile(2, 0, P, BESIDE[6:])
            with dve.Fori(0, TILES // 2 - 2) as j:
                proj_tile(2 * j + 3, 1, P)
                proj_tile(2 * j + 4, 0, P)
            proj_tile(TILES - 2, 1, P)
            proj_tile(TILES - 1, 0, P, last=True)
            for s in LATE:
                mix(s, 0, DEC)
            for part in range(11):
                topk(0, 0, part, 0)
            dve.wait_ge(st_out, 16 * 3)
            for t in (ct[:, :, :], mb[:, :], mrow[:, :], ktw[:, 0:WIN], vprev[:, :]):
                V.memset(t, 0.0)
            dve.drain()
            V.memset(vx[:, :, 128:129], 1.0)
            tile(0, DEC, (1, P))
            with dve.Fori(0, TILES - 2) as j:
                tile(j + 1, P, (j + 2, P))
            tile(TILES - 1, P, None)
            weigh(heads_before(TILES) - 1, 1)
            finish(TILES - 1)

        @block.tensor
        def _(pe):
            T = nc.tensor

            def transpose1(m, b, n):
                pe.wait_ge(h1_ready, m + 1)
                if not (isinstance(m, int) and m == 0):
                    pe.wait_ge(hT1_act, m)
                    pe.wait_ge(hT1_dve, m)
                for k in range(DC):
                    last = T.transpose(h2p[:, k * P:k * P + n], h1[b][0:n, k * P:(k + 1) * P], ident[0:n, 0:n])
                last.then_inc(h1_transposed, 1)

            def project(m, b, n, c):
                if c == 0:
                    pe.wait_ge(hT1_act, m + 1)
                    pe.wait_ge(hT1_dve, m + 1)
                first = isinstance(m, int) and m == 0
                if first:
                    pe.wait_ge(win_in[c], 16)
                if not (first and c < 2):
                    pe.wait_ge(chunk_dve if c % 2 else chunk_act, 3 * m + c // 2)
                for k in range(DC):
                    last = T.matmul(pbank[c][0:n, :], hT1[b][:, k, 0:n], win_s[c][:, k, :], start=k == 0, stop=k == DC - 1)
                last.then_inc(chunk_ready, 1)

            def proj_tile(m, b, n, beside=None, last=False):
                for c in range(6):
                    if c == 3 and not last:
                        transpose1(m + 1, 1 - b, P)
                    project(m, b, n, c)
                    for s in beside[c] if beside else ():
                        mix(s, 0, DEC)

            def transpose_state():
                for a in range(2):
                    last = T.transpose(mx[:, 3, a * NK:(a + 1) * NK], h2[:, a * P:(a + 1) * P], ident[:, :])
                last.then_inc(keysT_ready, 1)
                pe.wait_ge(state_in, 16 * 6)
                for h in range(MH):
                    T.transpose(mx[:, 0, h * P:(h + 1) * P], cat[:, h * P:(h + 1) * P], ident[:, :])
                T.transpose(mx[:, 1, 0:MH], cat[0:MH, 512:640], ident[0:MH, 0:MH])
                T.transpose(mx[:, 2, 0:P], cat[:, 640:768], ident[:, :]).then_inc(stateT_ready, 1)
                pe.wait_ge(state_set, 1)

            def store_state(count):
                pe.wait_ge(state_ready, 1 if count == 1 else TILES)
                pe.wait_ge(sc_ready, 1 if count == 1 else TILES)
                for h in range(MH):
                    T.transpose(mx[:, 0, h * P:(h + 1) * P], ct[:, h, 0:MD], ident[:, :])
                T.transpose(mx[0:MH, 1, 0:P], ct[:, :, MD:MD + 1].rearrange("p h a -> p (h a)"), ident[:, :]).then_inc(st_ready, 1)

            def mix(step, m, n):
                s, i = step
                if s == "qk_transpose":
                    pe.wait_ge(gates_ready, m + 1)
                    if not (isinstance(m, int) and m == 0):
                        pe.wait_ge(sc_ready, m)
                    if isinstance(m, int) and m == 1:
                        pe.wait_ge(st_copied, 1)
                    for a, off in ((0, OFF_Q), (1, OFF_K)):
                        for h in range(MH):
                            last = T.transpose(mx[:, 2 + a, h * P:h * P + n], pj[0:n, off + h * MD:off + (h + 1) * MD], ident[0:n, 0:n])
                    last.then_inc(qk_transposed, 1)
                elif s == "gate_sums":
                    pe.wait_ge(lf_ready, m + 1)
                    T.matmul(bcol[0:n, :], triu[0:n, 0:n], lf[0:n, 0, :], start=True, stop=True)
                    T.matmul(blast, ones[0:n, :], lf[0:n, 0, :], start=True, stop=True)
                    T.matmul(brow[:, 0:n], lf[0:n, 0, :], triu[0:n, 0:n], start=True, stop=True)
                    T.matmul(arow[:, 0:n], lf[0:n, 1, :], triu[0:n, 0:n], start=True, stop=False)
                    T.matmul(arow[:, 0:n], g8[0:n, 0:4], ident[0:n, 0:n], start=False, stop=True).then_inc(sums_ready, 1)
                    pe.wait_ge(mqT_ready, m + 1)
                    pe.wait_ge(mkT_ready, m + 1)
                    for h in range(MH):
                        last = T.matmul(mx[0:n, 2, h * P:h * P + n], qkT[:, 4 + h, 0:n], qkT[:, h, 0:n], start=True, stop=True)
                    last.then_inc(qk_ready, 1)
                elif s == "spread_max":
                    pe.wait_ge(grow_ready, m + 1)
                    gb = mx[0:n, 1, :].rearrange("p (h t) -> p h t", h=MH)[:, :, 0:n]
                    T.matmul(gb, ident[0:n, 0:n], dmask[0:n, 0:n].unsqueeze(1).broadcast_to([n, MH, n]), start=True, stop=False)
                    for h in range(MH):
                        T.matmul(gb[:, h, :], ident[0:MH, h:h + 1].broadcast_to([MH, n]), rows[:, 2, 0:n], start=False, stop=h == MH - 1)
                    T.matmul(gcol[0:n, :], rows[:, 2, 0:n], ident[0:MH, 0:MH], start=True, stop=True)
                    for h in range(MH):
                        last = T.matmul(glast[:, h:h + 1], ident[0:MH, h:h + 1].broadcast_to([MH, P]), rows[:, 2, n - 1:n], start=True, stop=True)
                    last.then_inc(gb_ready, 1)
                elif s == "mlstm_products":
                    pe.wait_ge(wT_ready, m + 1)
                    pe.wait_ge(exparg_ready, m + 1)
                    for h in range(MH):
                        T.matmul(mx[0:n, h // 2, h % 2 * 129:h % 2 * 129 + 129], wT[0:n, h, 0:n], vx[0:n, h, :], start=True, stop=True)
                    for h in range(MH):
                        last = T.matmul(mx[0:n, 2 + h // 2, h % 2 * 129:h % 2 * 129 + 129], qkT[:, h, 0:n], ct[:, h, :], start=True, stop=True)
                    last.then_inc(num_ready, 1)
                elif s == "mlstm_out":
                    pe.wait_ge(inter_ready, m + 1)
                    for h in range(MH):
                        last = T.matmul(mx[:, 2 + h // 2, h % 2 * 129:h % 2 * 129 + 129], pj[0:n, OFF_K + h * MD:OFF_K + (h + 1) * MD], vx[0:n, h, :], start=True, stop=True)
                    last.then_inc(dc_ready, 1)
                elif s == "attn_transpose":
                    pe.wait_ge(qr_ready, m + 1)
                    for j in range(GRP):
                        T.transpose(mx[:, 0, j * P:j * P + n], qr[0:n, j, :, :].rearrange("p g d -> p (g d)"), ident[0:n, 0:n])
                    T.transpose(mx[:, 1, 0:n], pj[0:n, OFF_SK:OFF_SV], ident[0:n, 0:n]).then_inc(swa_transposed, 1)
                elif s == "attn_scores":
                    pe.wait_ge(sqT_ready, m + 1)
                    pe.wait_ge(skT_ready, m + 1)
                    pe.wait_ge(state_ready, m + 1)
                    for h in range(QH):
                        r = slice(h // GRP * HD, h // GRP * HD + HD)
                        last = T.matmul(mx[0:n, h // 2, h % 2 * 256:h % 2 * 256 + WIN + n], qTs[r, h % GRP, 0:n], ktw[r, 0:WIN + n], start=True, stop=True)
                    last.then_inc(swa_scored, 1)
                elif s == "probs_transpose":
                    pe.wait_ge(probs_ready, m + 1)
                    for h in range(QH):
                        c = h % 2 * 256
                        T.transpose(mx[:, h // 2, c:c + n], sm[0:n, h, 0:WIN], ident[0:n, 0:n])
                        last = T.transpose(mx[0:n, h // 2, c + P:c + P + n], sm[0:n, h, WIN:WIN + n], ident[0:n, 0:n])
                    last.then_inc(probs_transposed, 1)
                elif s == "attn_out":
                    pe.wait_ge(pT_act, m + 1)
                    pe.wait_ge(pT_dve, m + 1)
                    for h in range(QH):
                        g = h // GRP * HD
                        T.matmul(mx[0:n, 0, h * HD:(h + 1) * HD], pT[:, h, 0, 0:n], vprev[:, g:g + HD], start=True, stop=False)
                        last = T.matmul(mx[0:n, 0, h * HD:(h + 1) * HD], pT[0:n, h, 1, 0:n], pj[0:n, OFF_SV + g:OFF_SV + g + HD], start=False, stop=True)
                    last.then_inc(attn_ready, 1)
                elif s in ("cat_transpose", "h2_transpose"):
                    rows_ = cat if s == "cat_transpose" else h2
                    pe.wait_ge(cat_ready if s == "cat_transpose" else h2_ready, m + 1)
                    for k in range(DC):
                        last = T.transpose(mx[:, k // 4, k % 4 * P:k % 4 * P + n], rows_[0:n, k * P:(k + 1) * P], ident[0:n, 0:n])
                    last.then_inc(rows_transposed, 1)
                elif s == "out_proj":
                    half, k0 = i // 4, i % 4 * 2
                    if i == 0:
                        pe.wait_ge(t8_act, 2 * m + 1)
                        pe.wait_ge(t8_dve, 2 * m + 1)
                        if isinstance(m, int) and m == 0:
                            pe.wait_ge(wout_in, 16)
                    for k in (k0, k0 + 1):
                        last = T.matmul(mx[0:n, 2 + half, :], t8[:, k, 0:n], wout_s[:, k, half * 512:half * 512 + 512], start=k == 0, stop=k == DC - 1)
                    if i == 7:
                        last.then_inc(mixed_ready, 1)
                elif s == "query":
                    if i == 0:
                        pe.wait_ge(t8_act, 2 * m + 2)
                        pe.wait_ge(t8_dve, 2 * m + 2)
                        if isinstance(m, int) and m == 0:
                            pe.wait_ge(wq_in, 16 * 4)
                    for k in range(DC):
                        last = T.matmul(mx[:, i // 4, i % 4 * P:i % 4 * P + n], wq_s[:, k, i * NK:(i + 1) * NK], t8[:, k, 0:n], start=k == 0, stop=k == DC - 1)
                    if i % 4 == 3:
                        last.then_inc(query_ready, 1)
                elif s == "score_keys":
                    if i == 0:
                        pe.wait_ge(qT_ready, 4 * (m + 1))
                    for c in range(QC // 2 * i, QC // 2 * (i + 1)):
                        if n == P:
                            out = mx[:, c // 4, c % 4 * NK:(c % 4 + 1) * NK]
                        else:
                            q, half = c // 2 % 4 * DEC, c // 8 * 2 + c % 2
                            out = mx[q:q + DEC, 0, half * NK:(half + 1) * NK]
                        last = T.matmul(out, qT[:, c, 0:n], kT[:, c % 2, :], start=True, stop=True)
                    if i == 1:
                        last.then_inc(keys_scored, 1)

            def tile(m, n, nxt):
                pe.wait_ge(x2_ready, m + 1)
                if not (isinstance(m, int) and m == 0):
                    pe.wait_ge(y_ready, m)
                for half in range(2):
                    last = T.matmul(acc[:, half * 512:half * 512 + 512], ident[:, :], xt[:, half * 512:half * 512 + 512], start=True, stop=False)
                last.then_inc(acc_set, 1)
                if isinstance(m, int) and m == 0:
                    for q in range(P // DEC):
                        for half in range(2):
                            cols = slice(half * 512, half * 512 + 512)
                            last = T.matmul(h2p[q * DEC:(q + 1) * DEC, cols], ident[0:DEC, 0:DEC], h2[0:DEC, cols], start=True, stop=True)
                    last.then_inc(h2p_set, 1)
                    for s in STEPS[:AHEAD]:
                        mix(s, *nxt)
                for h in range(heads_of(m)):
                    g = heads_before(m) + h
                    for k in range(TOPK):
                        pe.wait_ge(v_in[k % NV], 16 * (TOPK // NV * g + k // NV + 1))
                        pe.wait_ge(diag_ready, TOPK * g + k + 1)
                        end = h == heads_of(m) - 1 and k == TOPK - 1
                        for half in range(2):
                            last = T.matmul(acc[:, half * 512:half * 512 + 512], diag[:, k % NV, :],
                                            ring[:, NU + k % NV, half * 512:half * 512 + 512], start=False, stop=end)
                        last.then_inc(v_free, 1)
                        if end:
                            pe.drain().then_inc(acc_done, 1)
                        if nxt:
                            for s in step_at(TOPK * h + k, m):
                                mix(s, *nxt)

            pe.wait_ge(const_ready, 1)
            transpose1(0, 0, DEC)
            proj_tile(0, 0, DEC)
            transpose_state()
            proj_tile(1, 1, P, BESIDE[:6])
            proj_tile(2, 0, P, BESIDE[6:])
            with pe.Fori(0, TILES // 2 - 2) as j:
                proj_tile(2 * j + 3, 1, P)
                proj_tile(2 * j + 4, 0, P)
            proj_tile(TILES - 2, 1, P)
            proj_tile(TILES - 1, 0, P, last=True)
            for s in LATE:
                mix(s, 0, DEC)
            store_state(1)
            tile(0, DEC, (1, P))
            with pe.Fori(0, TILES - 2) as j:
                tile(j + 1, P, (j + 2, P))
            store_state(2)
            tile(TILES - 1, P, None)


_INS = ["x_prompt", "x_sample", "cache_swa_k", "cache_swa_v", "state_mlstm_c", "state_mlstm_n", "state_mlstm_m",
        "norm_mix_w", "w_in", "mlstm_if_bias", "mlstm_norm_w", "swa_sinks", "w_out", "norm_ffn_w", "peer_w_q",
        "peer_sub_keys_1", "peer_sub_keys_2", "peer_u", "peer_v", "norm_final_w"]
_OUTS = [(TILES * P, D), (1, 1, WIN, KVH, HD), (1, 1, WIN, KVH, HD), (1, 1, MH, MD, MD), (1, 1, MH, MD), (1, 1, MH),
         (1, 1, WIN, KVH, HD), (1, 1, WIN, KVH, HD), (1, 1, MH, MD, MD), (1, 1, MH, MD), (1, 1, MH)]


def rotation_table():
    pos = np.zeros(TILES * P, np.float32)
    pos[:DEC] = PAST + np.arange(DEC)
    pos[P:] = np.arange(SEQ)
    inv = np.float32(THETA) ** (-np.arange(ROT, dtype=np.float32) * np.float32(2.0) / np.float32(2 * ROT))
    ang = (pos[:, None] * inv[None, :].astype(np.float32)).astype(np.float32)
    return np.concatenate([np.cos(ang), np.sin(ang)], axis=1).astype(np.float32)


def kernel(**inputs):
    import concourse.bacc as _bacc
    from concourse.bass_utils import run_bass_kernel_spmd as _run

    nc = _bacc.Bacc("TRN2", target_bir_lowering=False, num_devices=1)
    arrays, args = {}, []
    for name in _INS + ["rotation"]:
        a = rotation_table() if name == "rotation" else np.ascontiguousarray(inputs[name])
        arrays[f"in_{name}_dram"] = a
        args.append(nc.dram_tensor(f"in_{name}_dram", a.shape, mybir.dt.from_np(a.dtype), kind="ExternalInput").ap())
    for i, shape in enumerate(_OUTS):
        args.append(nc.dram_tensor(f"out_{i}_dram", shape, F32, kind="ExternalOutput").ap())
    program(nc, *args)
    r = _run(nc, [arrays], core_ids=[0]).results[0]
    got = [r[f"out_{i}_dram"] for i in range(len(_OUTS))]
    y = got[0]
    return (y[P:].reshape(1, SEQ, D), y[:DEC].reshape(1, DEC, D), *got[1:])
```
